# Optimizing a Trainium2 kernel written in Bass

```python
import math
import jax, jax.numpy as jnp
from jax import lax
import numpy as np

D_MODEL = 1024
BATCH = 1
SEQ = 1024
DEPTH = 1
DEC_BATCH = 8
DEC_SEQ = 1
PAST_LEN = 8192
PAGE_SIZE = 128

EPS = 1e-6
D_S5 = D_MODEL // 2
S5_GROUP_CH = 16
S5_GROUPS = D_S5 // S5_GROUP_CH
S5_STATE = 64
D_LRU = D_MODEL // 2
LRU_HEADS = 8
LRU_BW = D_LRU // LRU_HEADS
CONV_W = 4
LRU_C = 8.0
PEER_HEADS = 8
PEER_DQ = 256
PEER_DK = PEER_DQ // 2
N_KEYS = 128
N_EXPERTS = N_KEYS * N_KEYS
PEER_TOPK = 16
PEER_BLOCK = 128
D_IN = D_S5 + 2 * D_LRU + 2 * D_MODEL
SPLITS = (D_S5, D_S5 + D_LRU, D_S5 + 2 * D_LRU, D_S5 + 2 * D_LRU + D_MODEL)

kernel_name = "hybrid_s5_rglru_peer_step"

def rmsnorm(x, g):
    xf = x.astype(jnp.float32)
    y = xf * lax.rsqrt(jnp.mean(xf * xf, axis=-1, keepdims=True) + EPS)
    return (y * g.astype(jnp.float32)).astype(x.dtype)

def linear_scan(a, b, h0):
    b = b.at[:, 0].add(a[:, 0] * h0)

    def comb(l, r):
        al, bl = l
        ar, br = r
        return ar * al, ar * bl + br

    _, h = lax.associative_scan(comb, (a, b), axis=1)
    return h

def complex_linear_scan(a_re, a_im, b_re, b_im, h0_re, h0_im):
    b_re = b_re.at[:, 0].add(a_re[:, 0] * h0_re - a_im[:, 0] * h0_im)
    b_im = b_im.at[:, 0].add(a_re[:, 0] * h0_im + a_im[:, 0] * h0_re)

    def comb(l, r):
        alr, ali, blr, bli = l
        arr, ari, brr, bri = r
        return (arr * alr - ari * ali,
                arr * ali + ari * alr,
                arr * blr - ari * bli + brr,
                arr * bli + ari * blr + bri)

    _, _, h_re, h_im = lax.associative_scan(comb, (a_re, a_im, b_re, b_im), axis=1)
    return h_re, h_im

def s5_branch(u, h0_re, h0_im, lam_re, lam_im, log_dt, b_re, b_im, c_re, c_im, d_skip, w_glu, b_glu):
    f32 = jnp.float32
    Bt, L, _ = u.shape
    uf = u.astype(f32)
    ug = uf.reshape(Bt, L, S5_GROUPS, S5_GROUP_CH)
    dt = jnp.exp(log_dt.astype(f32))[:, None]
    lr, li = lam_re.astype(f32), lam_im.astype(f32)
    mag = jnp.exp(lr * dt)
    abar_re = mag * jnp.cos(li * dt)
    abar_im = mag * jnp.sin(li * dt)
    nr, ni = abar_re - 1.0, abar_im
    den = lr * lr + li * li
    f_re = (nr * lr + ni * li) / den
    f_im = (ni * lr - nr * li) / den
    br, bi = b_re.astype(f32), b_im.astype(f32)
    bb_re = f_re[..., None] * br - f_im[..., None] * bi
    bb_im = f_re[..., None] * bi + f_im[..., None] * br
    bu_re = jnp.einsum('blgh,gph->blgp', ug, bb_re)
    bu_im = jnp.einsum('blgh,gph->blgp', ug, bb_im)
    a_re = jnp.broadcast_to(abar_re, bu_re.shape)
    a_im = jnp.broadcast_to(abar_im, bu_im.shape)
    h_re, h_im = complex_linear_scan(a_re, a_im, bu_re, bu_im,
                                     h0_re.astype(f32), h0_im.astype(f32))
    y = (jnp.einsum('blgp,ghp->blgh', h_re, c_re.astype(f32))
         - jnp.einsum('blgp,ghp->blgh', h_im, c_im.astype(f32)))
    y = y.reshape(Bt, L, D_S5) + d_skip.astype(f32) * uf
    z = jax.nn.gelu(y)
    out = z * jax.nn.sigmoid(z @ w_glu.astype(f32) + b_glu.astype(f32))
    return out.astype(u.dtype), h_re[:, -1], h_im[:, -1]

def rglru_branch(xr, yg, conv_buf, h0, conv_w, conv_b, w_a, b_a, w_x, b_x, lam):
    f32 = jnp.float32
    Bt, L, _ = xr.shape
    xp = jnp.concatenate([conv_buf.astype(xr.dtype), xr], axis=1)
    xc = conv_b + sum(xp[:, k:k + L] * conv_w[k] for k in range(CONV_W))
    new_buf = xp[:, -(CONV_W - 1):]
    xh = xc.astype(f32).reshape(Bt, L, LRU_HEADS, LRU_BW)
    r = jax.nn.sigmoid(jnp.einsum('blhi,hij->blhj', xh, w_a.astype(f32)) + b_a.astype(f32))
    i = jax.nn.sigmoid(jnp.einsum('blhi,hij->blhj', xh, w_x.astype(f32)) + b_x.astype(f32))
    log_a = -LRU_C * r * jax.nn.softplus(-lam.astype(f32))
    a = jnp.exp(log_a)
    b = jnp.sqrt(-jnp.expm1(2.0 * log_a)) * (i * xh)
    h = linear_scan(a.reshape(Bt, L, D_LRU), b.reshape(Bt, L, D_LRU), h0.astype(f32))
    out = h * jax.nn.gelu(yg.astype(f32))
    return out.astype(xr.dtype), h[:, -1], new_buf

def peer(x, w_q, sub_keys, u_tab, v_tab):
    Bt, L, D = x.shape
    T = Bt * L
    pad = (-T) % PEER_BLOCK
    xt = jnp.pad(x.reshape(T, D), ((0, pad), (0, 0)))
    xb = xt.reshape(-1, PEER_BLOCK, D)

    def block(xc):
        q = (xc @ w_q).reshape(PEER_BLOCK, PEER_HEADS, 2, PEER_DK)
        s = jnp.einsum('chsk,hsnk->chsn', q, sub_keys).astype(jnp.float32)
        sv, si = lax.top_k(s, PEER_TOPK)
        cand = sv[:, :, 0, :, None] + sv[:, :, 1, None, :]
        cidx = si[:, :, 0, :, None] * N_KEYS + si[:, :, 1, None, :]
        cs, sel = lax.top_k(cand.reshape(PEER_BLOCK, PEER_HEADS, PEER_TOPK * PEER_TOPK), PEER_TOPK)
        eidx = jnp.take_along_axis(cidx.reshape(PEER_BLOCK, PEER_HEADS, PEER_TOPK * PEER_TOPK), sel, axis=-1)
        g = jax.nn.softmax(cs, axis=-1)
        u = u_tab[eidx]
        act = jax.nn.gelu(jnp.einsum('chkd,cd->chk', u, xc).astype(jnp.float32))
        w = (g * act).astype(xc.dtype)
        return jnp.einsum('chk,chkd->cd', w, v_tab[eidx])

    out = lax.map(block, xb).reshape(-1, D)[:T]
    return out.reshape(Bt, L, D).astype(x.dtype)

def layer(x, h0_re, h0_im, lru_h0, conv_buf,
          w_in, lam_re, lam_im, log_dt, b_re, b_im, c_re, c_im, d_skip, w_glu, b_glu,
          conv_w, conv_b, w_a, b_a, w_x, b_x, lam, w_proj_a, w_proj_b, w_out,
          norm_mix, norm_ffn, w_q, sub_keys, u_tab, v_tab):
    h = rmsnorm(x, norm_mix)
    proj = h @ w_in
    u_s5, x_lru, y_lru, g_a, g_b = jnp.split(proj, SPLITS, axis=-1)
    a_out, s5_re, s5_im = s5_branch(u_s5, h0_re, h0_im, lam_re, lam_im, log_dt,
                                    b_re, b_im, c_re, c_im, d_skip, w_glu, b_glu)
    b_out, lru_h, new_buf = rglru_branch(x_lru, y_lru, conv_buf, lru_h0,
                                         conv_w, conv_b, w_a, b_a, w_x, b_x, lam)
    merged = (jax.nn.sigmoid(g_a) * (a_out @ w_proj_a)
              + jax.nn.sigmoid(g_b) * (b_out @ w_proj_b))
    x = x + merged @ w_out
    x = x + peer(rmsnorm(x, norm_ffn), w_q, sub_keys, u_tab, v_tab)
    return x, (s5_re, s5_im, lru_h, new_buf)

def setup_inputs(seed: int = 0) -> dict:
    key = jax.random.key(seed)
    ks = iter(jax.random.split(key, 48))
    f32 = jnp.float32

    def nrm(shape, scale):
        return scale * jax.random.normal(next(ks), shape, f32)

    n = jnp.arange(S5_STATE, dtype=f32)
    a0 = jax.random.uniform(next(ks), (DEPTH, LRU_HEADS, LRU_BW), f32, 0.9, 0.999)
    base = a0 ** (1.0 / LRU_C)
    return {
        "x_prompt": nrm((BATCH, SEQ, D_MODEL), 1.0),
        "x_sample": nrm((DEC_BATCH, DEC_SEQ, D_MODEL), 1.0),
        "state_s5_re": nrm((DEPTH, DEC_BATCH, S5_GROUPS, S5_STATE), 0.3),
        "state_s5_im": nrm((DEPTH, DEC_BATCH, S5_GROUPS, S5_STATE), 0.3),
        "state_lru_h": nrm((DEPTH, DEC_BATCH, D_LRU), 0.5),
        "state_conv": nrm((DEPTH, DEC_BATCH, CONV_W - 1, D_LRU), 1.0),
        "w_in": nrm((DEPTH, D_MODEL, D_IN), D_MODEL ** -0.5),
        "s5_lam_re": -0.5 + nrm((DEPTH, S5_GROUPS, S5_STATE), 0.01),
        "s5_lam_im": math.pi * n + nrm((DEPTH, S5_GROUPS, S5_STATE), 0.01),
        "s5_log_dt": jax.random.uniform(next(ks), (DEPTH, S5_GROUPS), f32, math.log(1e-3), math.log(1e-1)),
        "s5_b_re": nrm((DEPTH, S5_GROUPS, S5_STATE, S5_GROUP_CH), (2 * S5_GROUP_CH) ** -0.5),
        "s5_b_im": nrm((DEPTH, S5_GROUPS, S5_STATE, S5_GROUP_CH), (2 * S5_GROUP_CH) ** -0.5),
        "s5_c_re": nrm((DEPTH, S5_GROUPS, S5_GROUP_CH, S5_STATE), (2 * S5_STATE) ** -0.5),
        "s5_c_im": nrm((DEPTH, S5_GROUPS, S5_GROUP_CH, S5_STATE), (2 * S5_STATE) ** -0.5),
        "s5_d": 1.0 + nrm((DEPTH, D_S5), 0.1),
        "s5_w_glu": nrm((DEPTH, D_S5, D_S5), D_S5 ** -0.5),
        "s5_b_glu": nrm((DEPTH, D_S5), 0.01),
        "conv_w": nrm((DEPTH, CONV_W, D_LRU), CONV_W ** -0.5),
        "conv_b": nrm((DEPTH, D_LRU), 0.01),
        "lru_w_a": nrm((DEPTH, LRU_HEADS, LRU_BW, LRU_BW), LRU_BW ** -0.5),
        "lru_b_a": nrm((DEPTH, LRU_HEADS, LRU_BW), 0.01),
        "lru_w_x": nrm((DEPTH, LRU_HEADS, LRU_BW, LRU_BW), LRU_BW ** -0.5),
        "lru_b_x": nrm((DEPTH, LRU_HEADS, LRU_BW), 0.01),
        "lru_lam": jnp.log(base) - jnp.log1p(-base),
        "w_proj_a": nrm((DEPTH, D_S5, D_MODEL), D_S5 ** -0.5),
        "w_proj_b": nrm((DEPTH, D_LRU, D_MODEL), D_LRU ** -0.5),
        "w_out": nrm((DEPTH, D_MODEL, D_MODEL), D_MODEL ** -0.5),
        "norm_mix": 1.0 + nrm((DEPTH, D_MODEL), 0.05),
        "norm_ffn": 1.0 + nrm((DEPTH, D_MODEL), 0.05),
        "peer_w_q": nrm((DEPTH, D_MODEL, PEER_HEADS * PEER_DQ), D_MODEL ** -0.5),
        "peer_keys": nrm((DEPTH, PEER_HEADS, 2, N_KEYS, PEER_DK), PEER_DK ** -0.5),
        "peer_u": nrm((DEPTH, N_EXPERTS, D_MODEL), D_MODEL ** -0.5),
        "peer_v": nrm((DEPTH, N_EXPERTS, D_MODEL), PEER_HEADS ** -0.5),
        "norm_final": 1.0 + nrm((D_MODEL,), 0.05),
    }

def reference(x_prompt, x_sample, state_s5_re, state_s5_im, state_lru_h, state_conv,
              w_in, s5_lam_re, s5_lam_im, s5_log_dt, s5_b_re, s5_b_im, s5_c_re, s5_c_im,
              s5_d, s5_w_glu, s5_b_glu, conv_w, conv_b, lru_w_a, lru_b_a, lru_w_x, lru_b_x,
              lru_lam, w_proj_a, w_proj_b, w_out, norm_mix, norm_ffn,
              peer_w_q, peer_keys, peer_u, peer_v, norm_final):
    xp, xs = x_prompt, x_sample
    Bp = xp.shape[0]
    zp_re = jnp.zeros((Bp, S5_GROUPS, S5_STATE), jnp.float32)
    zp_im = jnp.zeros((Bp, S5_GROUPS, S5_STATE), jnp.float32)
    zp_h = jnp.zeros((Bp, D_LRU), jnp.float32)
    zp_conv = jnp.zeros((Bp, CONV_W - 1, D_LRU), xp.dtype)
    new_p = [[], [], [], []]
    new_s = [[], [], [], []]
    for l in range(DEPTH):
        params = (w_in[l], s5_lam_re[l], s5_lam_im[l], s5_log_dt[l], s5_b_re[l], s5_b_im[l],
                  s5_c_re[l], s5_c_im[l], s5_d[l], s5_w_glu[l], s5_b_glu[l],
                  conv_w[l], conv_b[l], lru_w_a[l], lru_b_a[l], lru_w_x[l], lru_b_x[l], lru_lam[l],
                  w_proj_a[l], w_proj_b[l], w_out[l], norm_mix[l], norm_ffn[l],
                  peer_w_q[l], peer_keys[l], peer_u[l], peer_v[l])
        xp, st_p = layer(xp, zp_re, zp_im, zp_h, zp_conv, *params)
        xs, st_s = layer(xs, state_s5_re[l], state_s5_im[l], state_lru_h[l], state_conv[l], *params)
        for j in range(4):
            new_p[j].append(st_p[j].astype(xp.dtype))
            new_s[j].append(st_s[j].astype(xs.dtype))
    y_prompt = rmsnorm(xp, norm_final)
    y_sample = rmsnorm(xs, norm_final)
    s5_re_p = jnp.stack(new_p[0])
    s5_im_p = jnp.stack(new_p[1])
    lru_h_p = jnp.stack(new_p[2])
    conv_p = jnp.stack(new_p[3])
    s5_re_s = jnp.stack(new_s[0])
    s5_im_s = jnp.stack(new_s[1])
    lru_h_s = jnp.stack(new_s[2])
    conv_s = jnp.stack(new_s[3])
    return (y_prompt, y_sample, s5_re_p, s5_im_p, lru_h_p, conv_p, s5_re_s, s5_im_s, lru_h_s, conv_s)


_drawn_inputs = setup_inputs


def setup_inputs(seed=0):
    import zlib

    import numpy as np

    out = dict(_drawn_inputs(seed))
    spreads = {}
    factors = {'s5_lam_re': 16.076, 's5_b_glu': 28.705, 'lru_b_a': 8.0, 'lru_b_x': 8.0}
    for name, (base, spread) in spreads.items():
        noise = np.random.default_rng([zlib.crc32(name.encode()), seed]).standard_normal(out[name].shape)
        drawn = base * np.exp(spread * noise) if base else spread * noise
        out[name] = __import__('jax').numpy.asarray(drawn.astype(out[name].dtype))
    for name, factor in factors.items():
        out[name] = (out[name] * factor).astype(out[name].dtype)
    return out
```

```python
from contextlib import ExitStack

import numpy as np

import concourse.bass as bass
from concourse import mybir

F32 = mybir.dt.float32
U32 = mybir.dt.uint32
I32 = mybir.dt.int32
ALU = mybir.AluOpType
ACT = mybir.ActivationFunctionType
AX = mybir.AxisListType.X

P = 128
D = 1024
KT = D // P
SEQ = 1024
NS = 8
TOK = SEQ + NS
CH = 3
N = TOK // CH
NP_LAST = N - NS
EPS = 1e-6
DB = 512
QT = DB // P
SJ = 16
CONV = 4
HEADS = 8
TOPK = 16
NKEY = 128
RING = 4
SLOTS = 28 + 4 + 8 + 8
ROWS = [(0, 128), (128, 128), (256, N - 256)]
XROWS = 9 * P
NEG = -3.0e38

U_XL, U_U, U_YL, U_GATE, U_GA, U_GB, U_GLU, U_MIX, U_OUT, UNITS = 0, 4, 8, 12, 20, 28, 36, 40, 48, 56
EVACS = 40


def slot_unit(l):
    return l if l < 12 else l + 8


class Arena:

    def __init__(self, tensor, at=0):
        self.tensor, self.at = tensor, at

    def take(self, *dims, dt=F32):
        n = int(np.prod(dims))
        v = self.tensor[:, self.at:self.at + n]
        self.at += n
        if dt != F32:
            v = v.bitcast(dt)
        if len(dims) == 2:
            v = v.rearrange("p (a b) -> p a b", a=dims[0])
        elif len(dims) == 3:
            v = v.rearrange("p (a b c) -> p a b c", a=dims[0], b=dims[1])
        return v


def build(nc, i_, o_):
    with ExitStack() as ctx:
        ARENA = 52600
        arena = ctx.enter_context(nc.sbuf_tensor("arena", [P, ARENA], F32))
        psum = ctx.enter_context(nc.psum_tensor("psum", [P, 8, 512], F32))
        x2_dram = nc.dram_tensor("x2_scratch", (XROWS, D), F32, kind="Internal").ap()
        idx_dram = nc.dram_tensor("idx_scratch", (NS, P), U32, kind="Internal").ap()
        g_dram = nc.dram_tensor("g_scratch", (NS, P), F32, kind="Internal").ap()
        hn_dram = nc.dram_tensor("hn_scratch", (NS, D), F32, kind="Internal").ap()

        def sem(name):
            return ctx.enter_context(nc.semaphore(name))

        T = Arena(arena)
        cosT = T.take(SJ, N)
        sinT = T.take(SJ, N)
        rc = T.take(2, N)
        rs = T.take(2, N)
        rv = T.take(2, N)
        rg = T.take(2, N)
        hb = T.take(3, 2, N)
        bT = T.take(2, QT, P)
        cT = T.take(2, SJ, 32)
        assert T.at >= KT * 2048
        xT = T.take(KT, N)
        hT = T.take(KT, N)
        ga = T.take(KT, N)
        gb = T.take(KT, N)
        uS = T.take(QT, N)
        xl = T.take(QT, N + CONV - 1)
        xc = T.take(QT, N)
        gy = T.take(QT, N)
        rT = T.take(QT, N)
        iT = T.take(QT, N)
        yS = T.take(QT, N)
        lru_at = T.at
        sT = T.take(QT, N)
        aT = T.take(QT, N)
        hl = T.take(QT, N)
        x_tok = Arena(arena, lru_at).take(len(ROWS), D)
        ring = T.take(RING, D)
        rstd = T.take(N)
        ident = T.take(P)
        ones = T.take(P)
        bd = T.take(QT, 2, P)
        nmix = T.take(KT)
        prm = T.take(40)
        mag = T.take(SJ)
        pre = T.take(2, SJ, NS)
        hS = T.take(2, SJ, NS)
        carr = T.take(2, SJ)
        lcar = T.take(QT)
        cSmp = T.take(QT, NS)
        sconv = T.take(QT, CONV - 1, NS)
        slru = T.take(QT, NS)
        dum = T.take(NS)
        assert T.at <= ARENA, T.at
        convb, dskip, bglu = prm[:, 0:4], prm[:, 4:8], prm[:, 8:12]
        bgate, lam, sp4 = prm[:, 12:20], prm[:, 20:24], prm[:, 24:28]
        convw = prm[:, 20 + 4 + 4:28 + 12]
        convw3 = T.take(QT)
        ztmp = T.take(QT, 6)
        assert T.at <= ARENA, T.at

        S = Arena(arena, 2 * SJ * N)
        lre, lim, ldt, th = (S.take(SJ) for _ in range(4))
        e0, e1, e2, e3, e4, e5 = (S.take(SJ) for _ in range(6))
        fre, fim = S.take(SJ), S.take(SJ)
        ei = S.take(SJ, dt=I32)
        TA, TB = 22, 16
        NT = TA + TB
        tau = S.take(NT)
        angles = S.take(2, SJ, NT)
        q0, q1 = angles[:, 0], angles[:, 1]
        q2 = S.take(SJ, NT)
        sc = S.take(2, SJ, NT)
        assert S.at <= 2 * SJ * N + 13 * N
        W = Arena(arena, lru_at - 3 * QT * N)
        braw = W.take(2, SJ, 16)
        bp = W.take(2, SJ, 32)
        b0, b1 = W.take(SJ, 16), W.take(SJ, 16)
        s0 = W.take(2, SJ, NS)
        assert W.at <= lru_at
        W.at = lru_at + D
        HJ = SJ // 4
        big, big2 = W.take(HJ, TA * TB), W.take(HJ, TA * TB)
        assert W.at <= lru_at + 3 * QT * N

        R = Arena(arena)
        wq = R.take(KT, 2048)
        R.take(0)
        uring = R.take(8, D)
        vring = R.take(8, D)
        keys = R.take(2 * HEADS, NKEY)
        x2n = R.take(D)
        hnn = R.take(D)
        hnc = R.take(D)
        hnT = R.take(KT, P)
        nffn = R.take(D)
        nfin = R.take(D)
        yo = R.take(D)
        dg = R.take(8, P)
        qS = R.take(2 * P)
        qT = R.take(2, P)
        sS = R.take(2, P)
        sM = R.take(2, P)
        cd = R.take(16, 16)
        cd2 = R.take(256)
        oh = R.take(2, 16, 16)
        sv = R.take(2, 16)
        ct = R.take(16)
        esh = R.take(16)
        en = R.take(16)
        esum = R.take(1)
        ersum = R.take(1)
        gn, gc = R.take(16), R.take(16)
        si = R.take(2, 16, dt=U32)
        pos = R.take(16, dt=U32)
        ab = R.take(2, 16, dt=U32)
        iab = R.take(2, 16)
        idxn = R.take(16, dt=U32)
        idxc = [R.take(16, dt=U32) for _ in range(2)]
        iota = R.take(16)
        acc = R.take(2, 4)
        ac = R.take(2, 4)
        wt = R.take(2, 4)
        ss, rt = R.take(1), R.take(1)
        ss2, rt2 = R.take(1), R.take(1)
        i8 = R.take(TOPK, HEADS, dt=U32)
        g8 = R.take(TOPK, HEADS)
        iS = R.take(HEADS, dt=U32)
        gS, accS, acS, wS = (R.take(HEADS) for _ in range(4))
        mk, mk2 = R.take(NS), R.take(NS)
        w8 = R.take(HEADS, NS)
        PEER_TOP = R.at
        IDENT_AT = lru_at + 3 * QT * N + RING * D + N
        assert PEER_TOP <= IDENT_AT, (PEER_TOP, IDENT_AT)

        par_in = sem("par_in")
        bd_in = sem("bd_in")
        const_ok = sem("const_ok")
        cz = sem("cz")
        halo_ok = sem("halo_ok")
        set_a = sem("set_a")
        set_b = sem("set_b")
        bp_ok = sem("bp_ok")
        bt_mm = sem("bt_mm")
        zrow = sem("zrow")
        x_in = sem("x_in")
        tok_in = sem("tok_in")
        slot_in = [sem(f"slot_in{k}") for k in range(RING)]
        sq_ok = sem("sq_ok")
        ss_ok = sem("ss_ok")
        ms_ok = sem("ms_ok")
        rt_ok = sem("rt_ok")
        hT_ok = sem("hT_ok")
        unit = sem("unit")
        evac = sem("evac")
        conv_ok = sem("conv_ok")
        tanh_ok = sem("tanh_ok")
        lru_ok = sem("lru_ok")
        bu_ok = sem("bu_ok")
        bu_read = sem("bu_read")
        h_ok = sem("h_ok")
        y_mm = sem("y_mm")
        y_ok = sem("y_ok")
        z_ok = sem("z_ok")
        a_ok = sem("a_ok")
        mix_ok = sem("mix_ok")
        x2_ok = sem("x2_ok")
        x2_out = sem("x2_out")
        st_out = sem("st_out")
        wq_in = [sem(f"wq_in{h}") for h in range(HEADS)]
        pk_in = sem("pk_in")
        p_const = sem("p_const")
        x2n_in = sem("x2n_in")
        x2n_free = sem("x2n_free")
        sq2_ok = sem("sq2_ok")
        ms2_ok = sem("ms2_ok")
        rt2_ok = sem("rt2_ok")
        hn_ok = sem("hn_ok")
        tr_ok = sem("tr_ok")
        hnT_ok = sem("hnT_ok")
        hnc_ok = sem("hnc_ok")
        q_mm, q_ev = sem("q_mm"), sem("q_ev")
        t_mm, t_ev = sem("t_mm"), sem("t_ev")
        s_mm, s_ev = sem("s_mm"), sem("s_ev")
        cs_ok, exp_ok = sem("cs_ok"), sem("exp_ok")
        g_ok = sem("g_ok")
        idx_ok = sem("idx_ok")
        idx_taken = sem("idx_taken")
        pool_at = sem("pool_at")
        dve_at = sem("dve_at")
        u_in = [sem(f"u_in{k}") for k in range(8)]
        v_in = [sem(f"v_in{k}") for k in range(8)]
        u_free = sem("u_free")
        v_free = sem("v_free")
        gelu_ok = sem("gelu_ok")
        w_ok = sem("w_ok")
        dg_ok = sem("dg_ok")
        pv_ok = sem("pv_ok")
        fs_ok, fm_ok, fr_ok = sem("fs_ok"), sem("fm_ok"), sem("fr_ok")
        yo_ok = sem("yo_ok")
        yo_free = sem("yo_free")
        y_out = sem("y_out")
        i8_ok, sc_out, sc_in = sem("i8_ok"), sem("sc_out"), sem("sc_in")
        w8_ok = sem("w8_ok")

        B = psum[:, 2:6, :]
        PB = [psum[:, 0, :], psum[:, 1, :]]
        YB = [psum[:, 6, :], psum[:, 7, :]]
        OUTB = [[psum[:, 0, :], psum[:, 1, :]], [psum[:, 6, :], psum[:, 7, :]], [psum[:, 2, :], psum[:, 3, :]]]
        PV = psum[:, 0:2, :]
        PQ, PT, PSC = psum[:, 2, 0:256], psum[:, 3, 0:256], psum[:, 4, 0:256]
        PX = psum[:, 6:8, :]

        block = ctx.enter_context(nc.Block())

        @block.sync
        def _(sp):
            sp.dma_start(xT, i_["xT"][:, :, 0:N]).then_inc(x_in, 16)
            weights = [i_["w_in"][m] for m in range(28)] + [i_["w_glu"][m] for m in range(4)] \
                + [i_["w_ab"][m] for m in range(8)] + [i_["w_out"][m] for m in range(8)]

            def load_weights(l, c):
                width = weights[l].shape[1]
                sp.dma_start(ring[:, l % RING, 0:width], weights[l]).then_inc(slot_in[l % RING], 16)

            for name, dst in (("lam_re", lre), ("lam_im", lim), ("prm", prm), ("nmix", nmix), ("b_raw", braw),
                              ("c_raw", cT), ("s5_0", s0), ("sconv", sconv), ("slru", slru), ("convw3", convw3)):
                sp.dma_start(dst, i_[name]).then_inc(par_in, 16)
            for g2 in range(2):
                sp.dma_start(ldt[64 * g2:64 * g2 + 64, :], i_["log_dt"][g2].partition_broadcast(64)).then_inc(par_in, 16)
            for l in range(RING):
                load_weights(l, 0)
            sp.dma_start(bd, i_["lru_bd"]).then_inc(bd_in, 16)
            sp.wait_ge(zrow, 1)
            sp.dma_start(x2_dram[TOK:XROWS, :], x_tok[0:XROWS - TOK, 0, :]).then_inc(x2_out, 16)

            def chunk(c, last):
                for l in range(RING, SLOTS):
                    if l == 12:
                        sp.wait_ge(hT_ok, KT * (c + 1))
                        if not last:
                            sp.dma_start(xT, i_["xT"][:, :, bass.ds((c + 1) * N, N)]).then_inc(x_in, 16)
                    sp.wait_ge(unit, UNITS * c + slot_unit(l - RING) + 1)
                    load_weights(l, c)
                    if l == SLOTS - 8:
                        sp.wait_ge(lru_ok, QT * (c + 1))
                        sp.wait_ge(x2_out, 16 + 48 * c)
                        for tt, (r0, rn) in enumerate(ROWS):
                            sp.dma_start(x_tok[0:rn, tt, :], i_["x_tok"][bass.ds(c * N + r0, rn), :]).then_inc(tok_in, 16)
                if last:
                    sp.wait_ge(y_mm, SJ * CH)
                    for h in range(HEADS):
                        sp.dma_start(wq[:, :, 256 * h:256 * h + 256], i_["w_q"][:, :, 256 * h:256 * h + 256]).then_inc(wq_in[h], 16)
                else:
                    for l in range(RING):
                        sp.wait_ge(unit, UNITS * c + slot_unit(SLOTS - RING + l) + 1)
                        load_weights(l, c)
                for tt, (r0, rn) in enumerate(ROWS):
                    sp.wait_ge(x2_ok, 6 * c + 2 * tt + 2)
                    sp.dma_start(x2_dram[bass.ds(c * N + r0, rn), :], x_tok[0:rn, tt, :]).then_inc(x2_out, 16)

            with sp.Fori(0, CH - 1) as c:
                chunk(c, False)
            chunk(CH - 1, True)
            sp.dma_start(o_["s5_s"], hS).then_inc(st_out, 16)
            sp.dma_start(o_["s5_p"], carr).then_inc(st_out, 16)
            sp.dma_start(o_["lru_p"], lcar).then_inc(st_out, 16)
            sp.dma_start(o_["lru_s"], slru).then_inc(st_out, 16)
            sp.dma_start(o_["conv_p"], xl[:, :, NP_LAST:NP_LAST + 3]).then_inc(st_out, 16)
            sp.dma_start(o_["conv_s"][:, :, 0:2, :], sconv[:, :, 1:3, :]).then_inc(st_out, 16)
            sp.dma_start(o_["conv_s"][:, :, 2, :], xl[:, :, 3 + NP_LAST:3 + N]).then_inc(st_out, 16)
            sp.wait_ge(x2_out, 16 + 48 * CH)
            sp.wait_ge(st_out, 16 * 7)
            sp.dma_start(keys, i_["keys"]).then_inc(pk_in, 16)
            sp.dma_start(nffn, i_["norm_ffn"].partition_broadcast(P)).then_inc(pk_in, 16)
            sp.dma_start(nfin, i_["norm_final"].partition_broadcast(P)).then_inc(pk_in, 16)
            sp.dma_start(x2n, x2_dram[0:P, :]).then_inc(x2n_in, 16)
            sp.sem_inc(yo_free, 1)
            with sp.Fori(0, SEQ // P) as i:
                sp.wait_ge(x2n_free, i + 1)
                sp.wait_ge(hn_ok, i + 1)
                sp.dma_start(x2n, x2_dram[bass.ds((i + 1) * P, P), :]).then_inc(x2n_in, 16)
                sp.wait_ge(yo_ok, i + 2)
                sp.dma_start(o_["y_prompt"][bass.ds(i * P, P), :], yo).then_inc(y_out, 16)
                sp.wait_ge(y_out, 16 * (i + 1))
                sp.sem_inc(yo_free, 1)
            sp.wait_ge(i8_ok, 1)
            sp.dma_start(idx_dram, i8[0:NS].rearrange("p k h -> p (k h)")).then_inc(sc_out, 16)
            sp.dma_start(g_dram, g8[0:NS].rearrange("p k h -> p (k h)")).then_inc(sc_out, 16)
            sp.dma_start(hn_dram, hnn[0:NS, :]).then_inc(sc_out, 16)
            sp.wait_ge(sc_out, 48)
            sp.dma_start(iS, idx_dram.rearrange("t (k h) -> (t k) h", h=HEADS)).then_inc(sc_in, 16)
            sp.dma_start(gS, g_dram.rearrange("t (k h) -> (t k) h", h=HEADS)).then_inc(sc_in, 16)
            for t in range(NS):
                sp.dma_start(hnc[16 * t:16 * t + 16, :], hn_dram[t].partition_broadcast(16)).then_inc(sc_in, 16)
            sp.wait_ge(yo_ok, SEQ // P + 2)
            sp.dma_start(o_["y_sample"], yo[0:NS, :]).then_inc(y_out, 16)
            sp.wait_ge(y_out, 16 * (SEQ // P + 1))

        @block.gpsimd
        def _(pool):
            pool.memset(ident, 0.0).then_inc(cz, 1)
            pool.memset(ones, 1.0).then_inc(const_ok, 1)
            pool.memset(xl[:, :, 0:CONV - 1], 0.0).then_inc(halo_ok, 1)
            pool.wait_ge(cz, 1)
            pool.affine_select(out=ident, in_=ident, compare_op=ALU.not_equal, fill=1.0, base=0,
                               pattern=[[-1, P]], channel_multiplier=1).then_inc(const_ok, 1)
            pool.iota(tau[:, 0:TA], [[TB, TA]], base=0, channel_multiplier=0,
                      allow_small_or_imprecise_dtypes=True).then_inc(const_ok, 1)
            pool.iota(tau[:, TA:NT], [[1, TB]], base=1, channel_multiplier=0,
                      allow_small_or_imprecise_dtypes=True).then_inc(const_ok, 1)

            pool.wait_ge(x2_out, 16 + 48 * CH)
            pool.wait_ge(st_out, 16 * 7)
            pool.iota(iota, [[1, 16]], base=0, channel_multiplier=0,
                      allow_small_or_imprecise_dtypes=True).then_inc(p_const, 1)
            pool.iota(mk, [[-16, NS]], base=0, channel_multiplier=1,
                      allow_small_or_imprecise_dtypes=True).then_inc(p_const, 1)

            def step(H, idxc):
                pool.wait_ge(idx_ok, H + 1)
                pool.sem_inc(pool_at, 1)
                pool.tensor_copy(idxc, idxn).then_inc(idx_taken, 1)
                pool.wait_ge(idx_taken, H + 1)
                pool.sem_inc(pool_at, 1)
                for b in range(4):
                    pool.wait_ge(u_free, 4 * H + b + 1)
                    pool.sem_inc(pool_at, 1)
                    for k in range(4 * b, 4 * b + 4):
                        pool.indirect_dma_start(uring[:, k % 8, :], None, i_["u"],
                                                bass.IndirectOffsetOnAxis(idxc[:, k:k + 1], 0)).then_inc(u_in[k % 8], 16)
                    pool.wait_ge(v_free, 4 * H + b + 1)
                    pool.sem_inc(pool_at, 1)
                    for k in range(4 * b, 4 * b + 4):
                        pool.indirect_dma_start(vring[:, k % 8, :], None, i_["v"],
                                                bass.IndirectOffsetOnAxis(idxc[:, k:k + 1], 0)).then_inc(v_in[k % 8], 16)

            with pool.Fori(0, SEQ // P * HEADS // 2) as pair:
                step(2 * pair, idxc[0])
                step(2 * pair + 1, idxc[1])
            pool.wait_ge(sc_in, 16 * (2 + NS))
            HH = SEQ // P * HEADS
            pool.wait_ge(u_free, 4 * HH + 2)
            for h in range(HEADS):
                pool.indirect_dma_start(uring[:, h, :], None, i_["u"],
                                        bass.IndirectOffsetOnAxis(iS[:, h:h + 1], 0)).then_inc(u_in[h], 16)
            pool.wait_ge(v_free, 4 * HH + 2)
            for h in range(HEADS):
                pool.indirect_dma_start(vring[:, h, :], None, i_["v"],
                                        bass.IndirectOffsetOnAxis(iS[:, h:h + 1], 0)).then_inc(v_in[h], 16)

        @block.scalar
        def _(act):
            def af(out, in_, f, **kw):
                return nc.scalar.activation(out, in_, f, **kw)

            def norm(c):
                act.wait_ge(x_in, 16 * (c + 1))
                act.wait_ge(mix_ok, KT * c)
                af(ga, xT, ACT.Square).then_inc(sq_ok, 1)
                act.wait_ge(ms_ok, c + 1)
                af(rstd, rstd, ACT.Sqrt).then_inc(rt_ok, 1)

            norm(0)
            act.wait_ge(set_a, 1)
            af(e1, e0, ACT.Tanh)
            af(ztmp[:, :, 1], ztmp[:, :, 0], ACT.Exp)
            act.drain()
            act.wait_ge(set_a, 2)
            af(sc, angles, ACT.Sin).then_inc(set_b, 1)

            def chunk(c, last):
                act.wait_ge(halo_ok, c + 1)
                for q in range(QT):
                    act.wait_ge(unit, UNITS * c + U_XL + q + 1)
                    af(xl[:, q, CONV - 1:], PB[q % 2][:, 0:N], ACT.Copy).then_inc(evac, 1)
                for q in range(QT):
                    act.wait_ge(unit, UNITS * c + U_U + q + 1)
                    af(uS[:, q, :], PB[q % 2][:, 0:N], ACT.Copy).then_inc(evac, 1)
                for q in range(QT):
                    act.wait_ge(unit, UNITS * c + U_YL + q + 1)
                    af(gy[:, q, :], PB[q % 2][:, 0:N], ACT.Gelu_apprx_tanh).then_inc(evac, 1)
                act.wait_ge(x2_out, 16 + 48 * c)
                for q in range(QT):
                    for s, dst in ((0, rT), (1, iT)):
                        act.wait_ge(unit, UNITS * c + U_GATE + 2 * q + s + 1)
                        af(dst[:, q, :], PB[s][:, 0:N], ACT.Sigmoid,
                           bias=bgate[:, 4 * s + q:4 * s + q + 1]).then_inc(evac, 1)
                act.drain()
                for q in range(QT):
                    af(rT[:, q, :], rT[:, q, :], ACT.Tanh, scale=sp4[:, q:q + 1])
                act.drain()
                af(sT, rT, ACT.Sqrt).then_inc(tanh_ok, 1)
                for m in range(2 * KT):
                    act.wait_ge(unit, UNITS * c + U_GA + m + 1)
                    dst = (ga if m < KT else gb)[:, m % KT, :]
                    af(dst, PB[m % 2][:, 0:N], ACT.Sigmoid).then_inc(evac, 1)
                for q in range(QT):
                    act.wait_ge(y_ok, QT * c + q + 1)
                    af(yS[:, q, :], yS[:, q, :], ACT.Gelu_apprx_tanh).then_inc(z_ok, 1)
                for q in range(QT):
                    act.wait_ge(unit, UNITS * c + U_GLU + q + 1)
                    af(rT[:, q, :], PB[q % 2][:, 0:N], ACT.Sigmoid, bias=bglu[:, q:q + 1]).then_inc(evac, 1)

            with act.Fori(0, CH - 1) as c:
                chunk(c, False)
                norm(c + 1)
            chunk(CH - 1, True)

            def score(H, h):
                act.wait_ge(q_mm, H + 1)
                af(qS, PQ, ACT.Copy).then_inc(q_ev, 1)
                act.wait_ge(t_mm, H + 1)
                af(qT.rearrange("p a b -> p (a b)"), PT, ACT.Copy).then_inc(t_ev, 1)
                act.wait_ge(s_mm, H + 1)
                af(sS.rearrange("p a b -> p (a b)"), PSC, ACT.Copy).then_inc(s_ev, 1)

            def soft(H):
                act.wait_ge(cs_ok, H + 1)
                af(en, esh, ACT.Exp, accum_out=esum).then_inc(exp_ok, 1)

            def prologue(i):
                act.wait_ge(x2n_in, 16 * (i + 1))
                act.wait_ge(hnc_ok, i)
                act.wait_ge(tr_ok, i)
                af(hnn, x2n, ACT.Square, accum_out=ss).then_inc(sq2_ok, 1)
                act.wait_ge(ms2_ok, i + 1)
                af(rt, ss, ACT.Sqrt).then_inc(rt2_ok, 1)
                act.wait_ge(tr_ok, i + 1)
                af(hnT.rearrange("p a b -> p (a b)"), PX.rearrange("p a b -> p (a b)"), ACT.Copy).then_inc(hnT_ok, 1)

            def step(H, soft_next=True):
                score(H + 1, None)
                for b in range(4):
                    act.wait_ge(u_free, 4 * H + b + 3)
                    af(ac[:, b % 2, :], acc[:, b % 2, :], ACT.Gelu_apprx_tanh).then_inc(gelu_ok, 1)
                    act.wait_ge(w_ok, 4 * H + b + 1)
                    act.wait_ge(v_free, 4 * H + b + 1)
                    for k in range(4):
                        ins = af(dg[:, 4 * (b % 2) + k, :], ident, ACT.Copy, scale=wt[:, b % 2, k:k + 1])
                    ins.then_inc(dg_ok, 1)
                    if b == 0:
                        soft(H + 1)

            def final(i, rows):
                if rows == P:
                    act.wait_ge(v_free, 4 * HEADS * (i + 1) + 2)
                else:
                    act.wait_ge(pv_ok, 1)
                act.wait_ge(yo_free, i + 1)
                af(yo[0:rows], PV[0:rows].rearrange("p a b -> p (a b)"), ACT.Square, accum_out=ss2[0:rows]).then_inc(fs_ok, 1)
                act.wait_ge(fm_ok, i + 1)
                af(rt2[0:rows], ss2[0:rows], ACT.Sqrt).then_inc(fr_ok, 1)

            act.wait_ge(x2_out, 16 + 48 * CH)
            act.wait_ge(st_out, 16 * 7)
            act.wait_ge(pk_in, 48)
            act.wait_ge(const_ok, 4)
            act.wait_ge(mix_ok, KT * CH)
            prologue(0)
            score(0, 0)
            soft(0)
            with act.Fori(0, SEQ // P) as i:
                act.wait_ge(u_free, 32 * i + 2)
                act.wait_ge(hn_ok, i + 1)
                af(hnc, hnn, ACT.Copy).then_inc(hnc_ok, 1)
                with act.Fori(0, HEADS - 1) as h:
                    step(i * HEADS + h)
                prologue(i + 1)
                step(i * HEADS + HEADS - 1)
                final(i, P)
            HH = SEQ // P * HEADS
            for h in range(1, HEADS):
                score(HH + h, h)
                soft(HH + h)
            act.wait_ge(u_free, 4 * HH + 3)
            af(acS, accS, ACT.Gelu_apprx_tanh).then_inc(gelu_ok, 1)
            final(SEQ // P, NS)

        @block.vector
        def _(dve):
            V = nc.vector

            def tt(out, a, b, op, *incs):
                ins = V.tensor_tensor(out, a, b, op)
                return ins

            def ts(out, a, s1, s2=None, op0=ALU.mult, op1=ALU.add):
                if s2 is None:
                    return V.tensor_scalar(out, a, s1, None, op0)
                return V.tensor_scalar(out, a, s1, s2, op0, op1)

            def chain(*steps):
                for f in steps:
                    f()
                    dve.drain()

            def norm(c):
                if isinstance(c, int):
                    dve.wait_ge(par_in, 16 * 12)
                dve.wait_ge(ss_ok, c + 1)
                ts(rstd, YB[0][:, 0:N], 1.0 / D, EPS).then_inc(ms_ok, 1)
                dve.wait_ge(rt_ok, c + 1)
                V.reciprocal(rstd, rstd)
                dve.drain()
                for k in range(KT):
                    V.scalar_tensor_tensor(out=hT[:, k], in0=xT[:, k], scalar=nmix[:, k:k + 1], in1=rstd,
                                           op0=ALU.mult, op1=ALU.mult).then_inc(hT_ok, 1)

            norm(0)
            dve.memset(x_tok[:, 0, :], 0.0).then_inc(zrow, 1)
            dve.memset(carr, 0.0)
            dve.memset(lcar, 0.0)
            dve.memset(bp, 0.0)
            dve.wait_ge(par_in, 16 * 12)
            dve.wait_ge(const_ok, 4)
            LN2H, LN2L = 0.693359375, -2.12194440e-4
            MAGIC = 12582912.0
            chain(
                lambda: ts(e0, ldt, -87.0, 88.0, ALU.max, ALU.min),
                lambda: ts(e1, e0, 1.4426950408889634, MAGIC, ALU.mult, ALU.add),
                lambda: ts(e1, e1, MAGIC, None, ALU.subtract),
                lambda: V.scalar_tensor_tensor(out=e2, in0=e1, scalar=-LN2H, in1=e0, op0=ALU.mult, op1=ALU.add),
                lambda: V.scalar_tensor_tensor(out=e2, in0=e1, scalar=-LN2L, in1=e2, op0=ALU.mult, op1=ALU.add),
                lambda: ts(e3, e2, 1.0 / 5040, 1.0 / 720),
            )
            for coef in (1.0 / 120, 1.0 / 24, 1.0 / 6, 0.5, 1.0, 1.0):
                chain(lambda: tt(e3, e3, e2, ALU.mult), lambda: ts(e3, e3, 1.0, coef))
            chain(
                lambda: ts(e1, e1, 127.0, 8388608.0, ALU.add, ALU.mult),
                lambda: V.tensor_copy(ei, e1),
                lambda: tt(e5, e3, ei.bitcast(F32), ALU.mult),
                lambda: tt(th, lim, e5, ALU.mult),
                lambda: tt(e0, lre, e5, ALU.mult),
                lambda: ts(e0, e0, -0.5),
            )
            zl = [ztmp[:, :, k] for k in range(6)]
            chain(
                lambda: ts(zl[2], lam, -1.0),
                lambda: tt(zl[3], lam, zl[2], ALU.min),
                lambda: V.tensor_copy(zl[0], zl[3]),
                lambda: ts(zl[5], zl[2], 0.0, None, ALU.max),
            )
            dve.sem_inc(set_a, 1)
            def bt3(a):
                return a.unsqueeze(2).to_broadcast([P, SJ, NT])
            taub = tau.unsqueeze(1).to_broadcast([P, SJ, NT])
            C1, C2 = 6.28125, 0.0019350051879882812
            C3 = 6.283185307179586 - C1 - C2
            chain(
                lambda: ts(e2, th, 4097.0),
                lambda: tt(e3, e2, th, ALU.subtract),
                lambda: tt(e3, e2, e3, ALU.subtract),
                lambda: tt(e4, th, e3, ALU.subtract),
                lambda: tt(q0, bt3(e3), taub, ALU.mult),
                lambda: tt(q1, bt3(e4), taub, ALU.mult),
                lambda: tt(q2, q0, q1, ALU.add),
                lambda: ts(q2, q2, 1.0 / 6.283185307179586, MAGIC),
                lambda: ts(q2, q2, MAGIC, None, ALU.subtract),
                lambda: V.scalar_tensor_tensor(out=q0, in0=q2, scalar=-C1, in1=q0, op0=ALU.mult, op1=ALU.add),
                lambda: V.scalar_tensor_tensor(out=q0, in0=q2, scalar=-C2, in1=q0, op0=ALU.mult, op1=ALU.add),
                lambda: V.scalar_tensor_tensor(out=q0, in0=q2, scalar=-C3, in1=q0, op0=ALU.mult, op1=ALU.add),
                lambda: tt(q0, q0, q1, ALU.add),
                lambda: ts(q1, q0, 1.5707963267948966, None, ALU.add),
                lambda: ts(q2, q1, 3.1415925, -6.283185307179586, ALU.is_gt, ALU.mult),
                lambda: tt(q1, q1, q2, ALU.add),
                lambda: ts(q0, q0, -3.1415925, 3.1415925, ALU.max, ALU.min),
                lambda: ts(q1, q1, -3.1415925, 3.1415925, ALU.max, ALU.min),
            )
            dve.sem_inc(set_a, 1)
            dve.wait_ge(set_b, 1)
            chain(
                lambda: ts(e2, e1, 1.0, None, ALU.add),
                lambda: V.reciprocal(e2, e2),
                lambda: ts(mag, e2, 2.0, -1.0),
            )
            chain(
                lambda: ts(zl[2], zl[1], 2.0, None, ALU.add),
                lambda: V.reciprocal(zl[2], zl[2]),
                lambda: tt(zl[2], zl[1], zl[2], ALU.mult),
                lambda: tt(zl[3], zl[2], zl[2], ALU.mult),
                lambda: ts(zl[4], zl[3], 1.0 / 15, 1.0 / 13),
            )
            for m in (11, 9, 7, 5, 3, 1):
                chain(lambda: tt(zl[4], zl[4], zl[3], ALU.mult), lambda: ts(zl[4], zl[4], 1.0, 1.0 / m))
            chain(
                lambda: tt(zl[4], zl[4], zl[2], ALU.mult),
                lambda: ts(zl[4], zl[4], 2.0),
                lambda: tt(zl[4], zl[4], zl[5], ALU.add),
                lambda: ts(sp4, zl[4], 4.0),
            )
            a_re, a_im, den = e0, e1, e2
            chain(
                lambda: tt(a_re, mag, sc[:, 1, :, TA], ALU.mult),
                lambda: tt(a_im, mag, sc[:, 0, :, TA], ALU.mult),
                lambda: tt(e3, lre, lre, ALU.mult),
                lambda: tt(e4, lim, lim, ALU.mult),
                lambda: tt(den, e3, e4, ALU.add),
                lambda: V.reciprocal(den, den),
                lambda: ts(e5, a_re, 1.0, None, ALU.subtract),
                lambda: tt(e3, e5, lre, ALU.mult),
                lambda: tt(e4, a_im, lim, ALU.mult),
                lambda: tt(e3, e3, e4, ALU.add),
                lambda: tt(fre, e3, den, ALU.mult),
                lambda: tt(e3, a_im, lre, ALU.mult),
                lambda: tt(e4, e5, lim, ALU.mult),
                lambda: tt(e3, e3, e4, ALU.subtract),
                lambda: tt(fim, e3, den, ALU.mult),
            )
            def over(a, n):
                return a.unsqueeze(2).to_broadcast([P, SJ, n])
            for part, (x, y, op) in enumerate(((0, 1, ALU.subtract), (1, 0, ALU.add))):
                tt(b0, over(fre, 16), braw[:, x], ALU.mult)
                tt(b1, over(fim, 16), braw[:, y], ALU.mult)
                dve.drain()
                for g2 in range(2):
                    r = slice(64 * g2, 64 * g2 + 64)
                    tt(bp[r, part, :, 16 * g2:16 * g2 + 16], b0[r], b1[r], op)
                dve.drain()
            ts(cT[:, 1], cT[:, 1], -1.0)
            dve.drain()
            dve.sem_inc(bp_ok, 1)
            for part, (x, y, op) in enumerate(((0, 1, ALU.subtract), (1, 0, ALU.add))):
                w0, w1 = b0[:, :, 0:NS], b1[:, :, 0:NS]
                tt(w0, over(a_re, NS), s0[:, x], ALU.mult)
                tt(w1, over(a_im, NS), s0[:, y], ALU.mult)
                dve.drain()
                tt(pre[:, part], w0, w1, op)
                dve.drain()
            for q in range(QT):
                for k in range(CONV - 1):
                    if k == 0:
                        ts(cSmp[:, q], sconv[:, q, 0], convw[:, q:q + 1], convb[:, q:q + 1])
                    else:
                        V.scalar_tensor_tensor(out=cSmp[:, q], in0=sconv[:, q, k], scalar=convw[:, 4 * k + q:4 * k + q + 1],
                                               in1=cSmp[:, q], op0=ALU.mult, op1=ALU.add)
                    dve.drain()
            for quarter in range(SJ // HJ):
                js = slice(HJ * quarter, HJ * quarter + HJ)

                def small(part, axis, js=js):
                    v = sc[:, part, js, 0:TA] if axis == 0 else sc[:, part, js, TA:NT]
                    return v.unsqueeze(3 if axis == 0 else 2).to_broadcast([P, HJ, TA, TB])
                b4 = [x.rearrange("p j (a b) -> p j a b", a=TA) for x in (big, big2)]
                for dst, (p0, p1), (p2, p3), op in ((cosT, (1, 1), (0, 0), ALU.subtract),
                                                    (sinT, (0, 1), (1, 0), ALU.add)):
                    tt(b4[0], small(p0, 0), small(p1, 1), ALU.mult)
                    tt(b4[1], small(p2, 0), small(p3, 1), ALU.mult)
                    dve.drain()
                    tt(dst[:, js], big[:, :, 0:N], big2[:, :, 0:N], op)
                    dve.drain()
            dve.wait_ge(bt_mm, 1)
            for part in range(2):
                V.tensor_copy(bT[:, part].rearrange("p a b -> p (a b)"), psum[:, 2 + part, :])
            dve.drain()
            dve.sem_inc(bp_ok, 1)

            def two(a):
                return a.unsqueeze(1).to_broadcast([P, 2, N])

            def conv(c, q, last):
                dve.wait_ge(evac, EVACS * c + U_XL + q + 1)
                ts(xc[:, q], xl[:, q, 0:N], convw[:, q:q + 1], convb[:, q:q + 1])
                dve.drain()
                for k in range(1, CONV):
                    w = convw[:, 4 * k + q:4 * k + q + 1] if k < CONV - 1 else convw3[:, q:q + 1]
                    V.scalar_tensor_tensor(out=xc[:, q], in0=xl[:, q, k:k + N], scalar=w, in1=xc[:, q],
                                           op0=ALU.mult, op1=ALU.add)
                    dve.drain()
                if last:
                    V.scalar_tensor_tensor(out=xc[:, q, NP_LAST:N], in0=xl[:, q, 3 + NP_LAST:3 + N],
                                           scalar=convw3[:, q:q + 1], in1=cSmp[:, q], op0=ALU.mult, op1=ALU.add)
                    dve.drain()
                dve.sem_inc(conv_ok, 1)

            def s5(c, j, last):
                even = 2 * (j % 2)
                bu = B[:, even:even + 2, 0:N]
                h = hb[:, j % 3]
                n = NP_LAST if last else N
                dve.wait_ge(bu_ok, SJ * c + j + 1)
                tt(rc, bu, two(cosT[:, j]), ALU.mult)
                if last:
                    tt(hS[:, :, j], pre[:, :, j], bu[:, :, NP_LAST:N], ALU.add)
                tt(rs, bu, two(sinT[:, j]), ALU.mult).then_inc(bu_read, 1)
                dve.drain()
                tt(rv[:, 0], rc[:, 0], rs[:, 1], ALU.add)
                tt(rv[:, 1], rc[:, 1], rs[:, 0], ALU.subtract)
                dve.drain()
                m = mag[:, j:j + 1].to_broadcast([P, n])
                for part in range(2):
                    V.tensor_tensor_scan(rg[:, part, 0:n], m, rv[:, part, 0:n], carr[:, part, j:j + 1], ALU.mult, ALU.add)
                dve.drain()
                tt(rc[:, :, 0:n], rg[:, :, 0:n], cosT[:, j, 0:n].unsqueeze(1).to_broadcast([P, 2, n]), ALU.mult)
                tt(rs[:, :, 0:n], rg[:, :, 0:n], sinT[:, j, 0:n].unsqueeze(1).to_broadcast([P, 2, n]), ALU.mult)
                dve.drain()
                if j >= 3:
                    dve.wait_ge(y_mm, SJ * c + j - 2)
                tt(h[:, 0, 0:n], rc[:, 0, 0:n], rs[:, 1, 0:n], ALU.subtract)
                tt(h[:, 1, 0:n], rc[:, 1, 0:n], rs[:, 0, 0:n], ALU.add)
                dve.drain()
                if last:
                    V.tensor_copy(h[:, :, n:N], hS[:, :, j])
                V.tensor_copy(carr[:, :, j:j + 1], h[:, :, n - 1:n])
                dve.drain()
                dve.sem_inc(h_ok, 1)

            def lru(c, q, last):
                n = NP_LAST if last else N
                if q == 0:
                    dve.wait_ge(tanh_ok, c + 1)
                r, s, i, a = rT[:, q], sT[:, q], iT[:, q], aT[:, q]
                ts(r, r, 1.0, None, ALU.add)
                tt(i, i, xc[:, q], ALU.mult)
                dve.drain()
                V.reciprocal(r, r)
                dve.drain()
                ts(a, r, 2.0, -1.0)
                tt(s, s, r, ALU.mult)
                dve.drain()
                V.scalar_tensor_tensor(out=i, in0=i, scalar=2.0, in1=s, op0=ALU.mult, op1=ALU.mult)
                dve.drain()
                V.tensor_tensor_scan(hl[:, q, 0:n], a[:, 0:n], i[:, 0:n], lcar[:, q:q + 1], ALU.mult, ALU.add)
                if last:
                    tt(dum, a[:, n:N], slru[:, q], ALU.mult)
                    dve.drain()
                    tt(hl[:, q, n:N], dum, i[:, n:N], ALU.add)
                dve.drain()
                V.tensor_copy(lcar[:, q:q + 1], hl[:, q, n - 1:n])
                if last:
                    V.tensor_copy(slru[:, q], hl[:, q, n:N])
                tt(gy[:, q], gy[:, q], hl[:, q], ALU.mult)
                dve.drain()
                dve.sem_inc(lru_ok, 1)

            def y_tile(c, q):
                dve.wait_ge(y_mm, SJ * c + 4 * q + 4)
                V.scalar_tensor_tensor(out=yS[:, q], in0=uS[:, q], scalar=dskip[:, q:q + 1], in1=YB[q % 2][:, 0:N],
                                       op0=ALU.mult, op1=ALU.add).then_inc(y_ok, 1)

            def chunk(c, last):
                for q in range(QT):
                    conv(c, q, last)
                if not last:
                    V.tensor_copy(xl[:, :, 0:3], xl[:, :, N:N + 3]).then_inc(halo_ok, 1)
                for j in range(SJ):
                    s5(c, j, last)
                    if j == 4:
                        dve.wait_ge(x2_out, 16 + 48 * c)
                    if 4 <= j < 8:
                        lru(c, j - 4, last)
                    if j in (8, 12):
                        y_tile(c, j // 4 - 2)
                y_tile(c, 2)
                y_tile(c, 3)
                for q in range(QT):
                    dve.wait_ge(evac, EVACS * c + U_GLU + q + 1)
                    tt(uS[:, q], yS[:, q], rT[:, q], ALU.mult).then_inc(a_ok, 1)
                for m in range(KT):
                    dve.wait_ge(unit, UNITS * c + U_MIX + m + 1)
                    even = 2 * (m % 2)
                    tt(ga[:, m], B[:, even, 0:N], ga[:, m], ALU.mult)
                    tt(gb[:, m], B[:, even + 1, 0:N], gb[:, m], ALU.mult)
                    dve.drain()
                    tt(hT[:, m], ga[:, m], gb[:, m], ALU.add).then_inc(mix_ok, 1)
                dve.wait_ge(unit, UNITS * (c + 1))
                dve.wait_ge(tok_in, 48 * (c + 1))
                for t, (r0, rn) in enumerate(ROWS):
                    for half in range(2):
                        v = x_tok[0:rn, t, 512 * half:512 * half + 512]
                        tt(v, OUTB[t][half][0:rn], v, ALU.add).then_inc(x2_ok, 1)

            with dve.Fori(0, CH - 1) as c:
                chunk(c, False)
                norm(c + 1)
            chunk(CH - 1, True)
            dve.wait_ge(x2_out, 16 + 48 * CH)
            dve.wait_ge(st_out, 16 * 7)
            dve.wait_ge(p_const, 2)
            dve.wait_ge(pk_in, 48)
            dve.sem_inc(u_free, 2)
            dve.sem_inc(yo_ok, 1)
            ts(mk2, mk, 0.0, None, ALU.is_ge)
            ts(mk, mk, 16.0, None, ALU.is_lt)
            dve.drain()
            tt(mk2, mk2, mk, ALU.mult)
            dve.drain()

            def topk(H):
                dve.wait_ge(s_ev, H + 1)
                dve.sem_inc(dve_at, 1)
                for s in range(2):
                    V.max(sv[:, s, 0:8], sS[:, s])
                dve.drain()
                for s in range(2):
                    V.max_index(si[:, s, 0:8], sv[:, s, 0:8], sS[:, s])
                    V.match_replace(sM[:, s], sv[:, s, 0:8], sS[:, s], NEG)
                dve.drain()
                for s in range(2):
                    V.max(sv[:, s, 8:16], sM[:, s])
                dve.drain()
                for s in range(2):
                    V.max_index(si[:, s, 8:16], sv[:, s, 8:16], sM[:, s])
                tt(cd, sv[:, 0].unsqueeze(2).to_broadcast([P, 16, 16]),
                   sv[:, 1].unsqueeze(1).to_broadcast([P, 16, 16]), ALU.add)
                dve.drain()
                cf = cd.rearrange("p a b -> p (a b)")
                V.max(ct[:, 0:8], cf)
                dve.drain()
                V.max_index(pos[:, 0:8], ct[:, 0:8], cf)
                V.match_replace(cd2, ct[:, 0:8], cf, NEG)
                dve.drain()
                V.max(ct[:, 8:16], cd2)
                dve.drain()
                V.max_index(pos[:, 8:16], ct[:, 8:16], cd2)
                ts(esh, ct, ct[:, 0:1], None, ALU.subtract).then_inc(cs_ok, 1)
                dve.drain()
                ts(ab[:, 0], pos, 4, None, ALU.logical_shift_right)
                ts(ab[:, 1], pos, 15, None, ALU.bitwise_and)
                dve.drain()
                for s in range(2):
                    tt(oh[:, s], ab[:, s].unsqueeze(2).to_broadcast([P, 16, 16]),
                       iota.unsqueeze(1).to_broadcast([P, 16, 16]), ALU.is_equal)
                dve.drain()
                for s in range(2):
                    tt(oh[:, s], oh[:, s], si[:, s].unsqueeze(1).to_broadcast([P, 16, 16]), ALU.mult)
                dve.drain()
                V.reduce_sum(iab, oh, AX)
                dve.drain()
                dve.wait_ge(idx_taken, H)
                V.scalar_tensor_tensor(out=idxn, in0=iab[:, 0], scalar=float(NKEY), in1=iab[:, 1],
                                       op0=ALU.mult, op1=ALU.add).then_inc(idx_ok, 1)

            def softmax(H):
                dve.wait_ge(exp_ok, H + 1)
                V.reciprocal(ersum, esum)
                dve.drain()
                ts(gn, en, ersum[:, 0:1])
                dve.drain()

            def prologue(i):
                dve.wait_ge(sq2_ok, i + 1)
                ts(ss, ss, 1.0 / D, EPS).then_inc(ms2_ok, 1)
                dve.wait_ge(rt2_ok, i + 1)
                V.reciprocal(rt, rt)
                dve.drain()
                V.scalar_tensor_tensor(out=hnn, in0=x2n, scalar=rt[:, 0:1], in1=nffn,
                                       op0=ALU.mult, op1=ALU.mult).then_inc(hn_ok, 1)

            def dots(H, b):
                for k in range(4 * b, 4 * b + 4):
                    dve.wait_ge(u_in[k % 8], 16 * (2 * H + k // 8 + 1))
                    u = uring[:, k % 8, :]
                    ins = V.tensor_tensor_reduce(out=u, in0=u, in1=hnc, scale=1.0, scalar=0.0, op0=ALU.mult,
                                                 op1=ALU.add, accum_out=acc[:, b % 2, k % 4:k % 4 + 1])
                ins.then_inc(u_free, 1)

            def weights(H, b):
                dve.wait_ge(gelu_ok, 4 * H + b + 1)
                tt(wt[:, b % 2], ac[:, b % 2], gc[:, 4 * b:4 * b + 4], ALU.mult).then_inc(w_ok, 1)

            def step(H):
                dve.drain()
                V.tensor_copy(gc, gn)
                dve.drain()
                dots(H, 0)
                weights(H, 0)
                topk(H + 1)
                dots(H, 1)
                weights(H, 1)
                softmax(H + 1)
                for b in (2, 3):
                    dots(H, b)
                    weights(H, b)

            def final(i, rows):
                dve.wait_ge(fs_ok, i + 1)
                ts(ss2[0:rows], ss2[0:rows], 1.0 / D, EPS).then_inc(fm_ok, 1)
                dve.wait_ge(fr_ok, i + 1)
                V.reciprocal(rt2[0:rows], rt2[0:rows])
                dve.drain()
                V.scalar_tensor_tensor(out=yo[0:rows], in0=PV[0:rows].rearrange("p a b -> p (a b)"),
                                       scalar=rt2[0:rows, 0:1], in1=nfin[0:rows],
                                       op0=ALU.mult, op1=ALU.mult).then_inc(yo_ok, 1)

            prologue(0)
            topk(0)
            softmax(0)
            with dve.Fori(0, SEQ // P) as i:
                dve.wait_ge(hnc_ok, i + 1)
                dve.sem_inc(dve_at, 1)
                with dve.Fori(0, HEADS - 1) as h:
                    step(i * HEADS + h)
                prologue(i + 1)
                step(i * HEADS + HEADS - 1)
                final(i, P)
            HH = SEQ // P * HEADS
            for h in range(HEADS):
                if h:
                    topk(HH + h)
                    softmax(HH + h)
                dve.wait_ge(idx_ok, HH + h + 1)
                V.tensor_copy(i8[:, :, h], idxn)
                V.tensor_copy(g8[:, :, h], gn)
                dve.drain()
                dve.sem_inc(idx_taken, 1)
            dve.sem_inc(i8_ok, 1)
            dve.wait_ge(sc_in, 16 * (2 + NS))
            for h in range(HEADS):
                dve.wait_ge(u_in[h], 16 * (2 * HH + 1))
                u = uring[:, h, :]
                ins = V.tensor_tensor_reduce(out=u, in0=u, in1=hnc, scale=1.0, scalar=0.0, op0=ALU.mult,
                                             op1=ALU.add, accum_out=accS[:, h:h + 1])
            ins.then_inc(u_free, 1)
            dve.wait_ge(gelu_ok, 4 * HH + 1)
            tt(wS, acS, gS, ALU.mult)
            dve.drain()
            tt(w8, wS.unsqueeze(2).to_broadcast([P, HEADS, NS]), mk2.unsqueeze(1).to_broadcast([P, HEADS, NS]),
               ALU.mult).then_inc(w8_ok, 1)
            final(SEQ // P, NS)

        @block.tensor
        def _(pe):
            mm = nc.tensor.matmul

            def norm(c):
                pe.wait_ge(x2_ok, 6 * c)
                pe.wait_ge(sq_ok, c + 1)
                for k in range(KT):
                    ins = mm(YB[0][:, 0:N], ones, ga[:, k], start=(k == 0), stop=(k == KT - 1))
                ins.then_inc(ss_ok, 1)

            pe.wait_ge(const_ok, 4)
            norm(0)
            pe.wait_ge(bp_ok, 1)
            for part in range(2):
                for j in range(SJ):
                    o = 32 * (j % 4)
                    ins = mm(psum[o:o + 32, 2 + part, P * (j // 4):P * (j // 4) + P], bp[:, part, j], ident,
                             start=True, stop=True)
            ins.then_inc(bt_mm, 1)
            pe.wait_ge(bd_in, 16)
            pe.wait_ge(par_in, 16 * 12)

            def slot(c, l):
                pe.wait_ge(slot_in[l % RING], 16 * (SLOTS // RING * c + l // RING + 1))
                return ring[:, l % RING, :]

            def project(c, n, l, rhs, k):
                w = slot(c, l)
                if n >= 2:
                    pe.wait_ge(evac, EVACS * c + n - 1)
                for t in range(k):
                    ins = mm(PB[n % 2][:, 0:N], w[:, P * t:P * t + P], rhs[:, t], start=(t == 0), stop=(t == k - 1))
                ins.then_inc(unit, 1)

            def s5_in(c, j):
                o = 32 * (j % 4)
                if j >= 2:
                    pe.wait_ge(bu_read, SJ * c + j - 1)
                pe.wait_ge(evac, EVACS * c + U_U + j // 4 + 1)
                for part in range(2):
                    ins = mm(B[:, 2 * (j % 2) + part, 0:N], bT[o:o + 32, part, j // 4], uS[o:o + 32, j // 4],
                             start=True, stop=True)
                ins.then_inc(bu_ok, 1)

            def s5_out(c, j):
                o, q = 32 * (j % 4), j // 4
                pe.wait_ge(h_ok, SJ * c + j + 1)
                if j % 4 == 0 and q >= 2:
                    pe.wait_ge(y_ok, QT * c + q - 1)
                for part in range(2):
                    ins = mm(YB[q % 2][o:o + 32, 0:N], cT[:, part, j], hb[:, j % 3, part], start=(part == 0), stop=(part == 1))
                ins.then_inc(y_mm, 1)

            def chunk(c):
                pe.wait_ge(hT_ok, KT * (c + 1))
                for n in range(U_GATE):
                    project(c, n, n, hT, KT)
                    if n == U_YL:
                        pe.wait_ge(bp_ok, 2)
                    if n > U_YL:
                        s5_in(c, n - U_YL - 1)
                for n in range(U_GATE, U_GA):
                    q, s = divmod(n - U_GATE, 2)
                    if s == 0:
                        pe.wait_ge(conv_ok, QT * c + q + 1)
                    pe.wait_ge(evac, EVACS * c + n - 1)
                    mm(PB[n % 2][:, 0:N], bd[:, q, s], xc[:, q], start=True, stop=True).then_inc(unit, 1)
                for m in range(2 * KT):
                    project(c, U_GA + m, U_YL + 4 + m, hT, KT)
                    if 3 + m < SJ:
                        s5_in(c, 3 + m)
                    s5_out(c, m)
                for q in range(QT):
                    if q == 0:
                        pe.wait_ge(z_ok, QT * (c + 1))
                    project(c, U_GLU + q, 28 + q, yS, QT)
                pe.wait_ge(lru_ok, QT * (c + 1))
                for m in range(KT):
                    w = slot(c, 32 + m)
                    if m == 0:
                        pe.wait_ge(bu_read, SJ * (c + 1))
                        pe.wait_ge(a_ok, QT * (c + 1))
                    if m >= 2:
                        pe.wait_ge(mix_ok, KT * c + m - 1)
                    for side, src in ((1, gy), (0, uS)):
                        for t in range(QT):
                            ins = mm(B[:, 2 * (m % 2) + side, 0:N], w[:, 512 * side + P * t:512 * side + P * t + P],
                                     src[:, t], start=(t == 0), stop=(t == QT - 1))
                    ins.then_inc(unit, 1)
                pe.wait_ge(evac, EVACS * (c + 1))
                pe.wait_ge(y_ok, QT * (c + 1))
                for k in range(KT):
                    w = slot(c, 40 + k)
                    pe.wait_ge(mix_ok, KT * (c + 1))
                    for t, (r0, rn) in enumerate(ROWS):
                        for half in range(2):
                            ins = mm(OUTB[t][half][0:rn], hT[:, k, r0:r0 + rn], w[:, 512 * half:512 * half + 512],
                                     start=(k == 0), stop=(k == KT - 1))
                    ins.then_inc(unit, 1)

            with pe.Fori(0, CH - 1) as c:
                chunk(c)
                norm(c + 1)
            chunk(CH - 1)

            pe.wait_ge(x2_ok, 6 * CH)
            pe.wait_ge(pk_in, 48)
            for h in range(HEADS):
                pe.wait_ge(wq_in[h], 16)
            pe.sem_inc(v_free, 2)

            def score(H, h):
                pe.wait_ge(q_ev, H)
                for k in range(KT):
                    ins = mm(PQ, hnT[:, k], wq[:, k, bass.ds(h * 256, 256)], start=(k == 0), stop=(k == KT - 1))
                ins.then_inc(q_mm, 1)
                pe.wait_ge(q_ev, H + 1)
                for s in range(2):
                    ins = nc.tensor.transpose(PT[:, P * s:P * s + P], qS[:, P * s:P * s + P], ident)
                ins.then_inc(t_mm, 1)
                pe.wait_ge(t_ev, H + 1)
                for s in range(2):
                    ins = mm(PSC[:, P * s:P * s + P], qT[:, s], keys[:, bass.ds(2 * h + s, 1), :].rearrange("p a b -> p (a b)"),
                             start=True, stop=True)
                ins.then_inc(s_mm, 1)

            def prologue(i):
                pe.wait_ge(hn_ok, i + 1)
                pe.wait_ge(hnT_ok, i)
                for k in range(KT):
                    ins = nc.tensor.transpose(PX[:, k // 4, P * (k % 4):P * (k % 4) + P], hnn[:, P * k:P * k + P], ident)
                ins.then_inc(tr_ok, 1)
                pe.wait_ge(hnT_ok, i + 1)

            def start_tile(i):
                pe.wait_ge(yo_ok, i + 1)
                pe.wait_ge(x2n_in, 16 * (i + 1))
                for half in range(2):
                    ins = mm(PV[:, half], ident, x2n[:, 512 * half:512 * half + 512], start=True, stop=False)
                ins.then_inc(x2n_free, 1)

            def step(H, hn, stop):
                score(H + 1, hn)
                for b in range(4):
                    pe.wait_ge(dg_ok, 4 * H + b + 1)
                    for k in range(4 * b, 4 * b + 4):
                        pe.wait_ge(v_in[k % 8], 16 * (2 * H + k // 8 + 1))
                        for half in range(2):
                            ins = mm(PV[:, half], dg[:, k % 8], vring[:, k % 8, 512 * half:512 * half + 512],
                                     start=False, stop=(stop and k == TOPK - 1))
                    ins.then_inc(v_free, 1)

            prologue(0)
            score(0, 0)
            with pe.Fori(0, SEQ // P) as i:
                start_tile(i)
                with pe.Fori(0, HEADS - 1) as h:
                    step(i * HEADS + h, h + 1, False)
                prologue(i + 1)
                step(i * HEADS + HEADS - 1, 0, True)
            HH = SEQ // P * HEADS
            for h in range(1, HEADS):
                pe.wait_ge(s_ev, HH + h)
                score(HH + h, h)
            pe.wait_ge(yo_ok, SEQ // P + 1)
            for half in range(2):
                mm(PV[0:NS, half], ident[:, 0:NS], x2n[:, 512 * half:512 * half + 512], start=True, stop=False)
            pe.wait_ge(w8_ok, 1)
            for h in range(HEADS):
                pe.wait_ge(v_in[h], 16 * (2 * HH + 1))
                for half in range(2):
                    ins = mm(PV[0:NS, half], w8[:, h], vring[:, h, 512 * half:512 * half + 512],
                             start=False, stop=(h == HEADS - 1))
            ins.then_inc(pv_ok, 1)


def kernel(**inputs):
    import concourse.bacc as bacc
    from concourse.bass_utils import run_bass_kernel_spmd

    a = {k: np.asarray(v) for k, v in inputs.items()}
    x = np.concatenate([a["x_prompt"][0], a["x_sample"][:, 0]], axis=0)

    def states(v):
        v = v.reshape((SJ, 2, 64) + v.shape[2:])
        return np.moveaxis(v, 0, 2).reshape((P, SJ) + v.shape[3:])

    def chans(v):
        v = v.reshape(v.shape[:-1] + (-1, P))
        return np.moveaxis(np.moveaxis(v, -1, 0), -1, 1)

    def tiles(w):
        k, m = w.shape
        return w.reshape(k // P, P, m // P, P).transpose(2, 1, 0, 3).reshape(m // P, P, k)

    w_in = tiles(a["w_in"][0])
    order = list(range(4, 8)) + list(range(0, 4)) + list(range(8, 28))
    gate = np.stack([a["lru_w_a"][0], a["lru_w_x"][0]])
    bd = np.zeros((P, QT, 2, P), np.float32)
    c_raw = np.zeros((P, 2, SJ, 32), np.float32)
    c_all = [states(a[n][0].transpose(0, 2, 1)) for n in ("s5_c_re", "s5_c_im")]
    for g2 in range(2):
        r = slice(64 * g2, 64 * g2 + 64)
        bd[r, :, :, r] = gate[:, g2::2].transpose(2, 1, 0, 3)
        for s in range(2):
            c_raw[r, s, :, 16 * g2:16 * g2 + 16] = c_all[s][r]
    conv_w = a["conv_w"][0]
    prm = np.concatenate([chans(a["conv_b"][0]), chans(a["s5_d"][0]), chans(a["s5_b_glu"][0]),
                          chans(a["lru_b_a"][0].reshape(-1)), chans(a["lru_b_x"][0].reshape(-1)),
                          chans(a["lru_lam"][0].reshape(-1)), np.zeros((P, QT), np.float32)]
                         + [chans(conv_w[k]) for k in range(3)], axis=1)
    ins = {
        "xT": chans(x), "x_tok": x, "w_in": w_in[order], "w_glu": tiles(a["s5_w_glu"][0]),
        "w_ab": np.concatenate([tiles(a["w_proj_a"][0]), tiles(a["w_proj_b"][0])], axis=2),
        "w_out": a["w_out"][0].reshape(KT, P, D),
        "lam_re": states(a["s5_lam_re"][0]), "lam_im": states(a["s5_lam_im"][0]),
        "log_dt": a["s5_log_dt"][0].reshape(SJ, 2).T,
        "b_raw": np.stack([states(a["s5_b_re"][0]), states(a["s5_b_im"][0])], axis=1),
        "c_raw": c_raw,
        "s5_0": np.stack([states(np.moveaxis(a[n][0], 0, 2)) for n in ("state_s5_re", "state_s5_im")], axis=1),
        "prm": prm, "convw3": chans(conv_w[3]), "nmix": chans(a["norm_mix"][0]),
        "sconv": chans(a["state_conv"][0].transpose(1, 0, 2)), "slru": chans(a["state_lru_h"][0]),
        "lru_bd": bd,
        "w_q": a["peer_w_q"][0].reshape(KT, P, 2048).transpose(1, 0, 2),
        "keys": a["peer_keys"][0].reshape(2 * HEADS, NKEY, P).transpose(2, 0, 1),
        "u": a["peer_u"][0], "v": a["peer_v"][0],
        "norm_ffn": a["norm_ffn"][0], "norm_final": a["norm_final"],
    }
    ins = {f"in_{k}": np.ascontiguousarray(v) for k, v in ins.items()}
    outs = {"y_prompt": (SEQ, D), "y_sample": (NS, D), "s5_s": (P, 2, SJ, NS), "s5_p": (P, 2, SJ),
            "lru_p": (P, QT), "lru_s": (P, QT, NS), "conv_p": (P, QT, 3), "conv_s": (P, QT, 3, NS)}
    nc = bacc.Bacc("TRN2", target_bir_lowering=False, num_devices=1)
    i_ = {k[3:]: nc.dram_tensor(k, v.shape, F32, kind="ExternalInput").ap() for k, v in ins.items()}
    o_ = {k: nc.dram_tensor(f"out_{k}", s, F32, kind="ExternalOutput").ap() for k, s in outs.items()}
    build(nc, i_, o_)
    res = run_bass_kernel_spmd(nc, [ins], core_ids=[0]).results[0]
    r = {k: np.asarray(res[f"out_{k}"]) for k in outs}

    def unstate(v):
        v = v.reshape((2, 64, SJ) + v.shape[2:])
        return np.moveaxis(v, 2, 0).reshape((32, 64) + v.shape[3:])

    s5p = [unstate(r["s5_p"][:, s])[None, None] for s in range(2)]
    s5s = [np.moveaxis(unstate(r["s5_s"][:, s]), 2, 0)[None] for s in range(2)]
    return (r["y_prompt"][None], r["y_sample"][:, None], s5p[0], s5p[1],
            r["lru_p"].T.reshape(1, 1, DB), r["conv_p"].transpose(2, 1, 0).reshape(1, 1, 3, DB),
            s5s[0], s5s[1], r["lru_s"].transpose(2, 1, 0).reshape(1, NS, DB),
            r["conv_s"].transpose(3, 2, 1, 0).reshape(1, NS, 3, DB))
```

```python
from contextlib import ExitStack

import numpy as np

import concourse.bass as bass
from concourse import mybir

F32 = mybir.dt.float32
U32 = mybir.dt.uint32
I32 = mybir.dt.int32
ALU = mybir.AluOpType
ACT = mybir.ActivationFunctionType
AX = mybir.AxisListType.X

P = 128
D = 1024
KT = D // P
SEQ = 1024
NS = 8
TOK = SEQ + NS
TILES = SEQ // P
C = 256
CH = SEQ // C
N = C + NS
SEG = 128
EPS = 1e-6
DB = 512
QT = DB // P
SJ = 16
CONV = 4
HEADS = 8
TOPK = 16
NKEY = 128
RING = 4
SLOTS = 28 + 4 + 8 + 8 + 16
NEG = -3.0e38

BT = HEADS * TOPK // 4
BC = 2 * BT
BS = BC + 5
ONPE = 3

U_XL, U_U, U_YL, U_GATE, U_GA, U_GB, U_GLU, U_MIX, U_OUT, U_Q, UNITS = 0, 4, 8, 12, 20, 28, 36, 40, 48, 56, 72
EVACS = 56

AT_GATE, AT_S5, AT_LRU, AT_GLU, AT_MIX, AT_OUT, AT_X2, AT_HN, AT_TR, AT_Q, AT_NORM = \
    6, 7, 23, 26, 27, 32, 37, 38, 39, 40, 65


def at_y(q):
    return AT_S5 + 4 * q + 6


def at_q(h):
    return AT_Q + 3 * h


def slot_unit(l):
    return l if l < 12 else l + 8


def hn_stored(c):
    return 32 * (c + 1) + (16 if isinstance(c, int) and c == CH - 1 else 0)


def columns(c):
    return C if isinstance(c, int) and c < CH - 1 else N


def need(engine, semaphore, value):
    if not isinstance(value, int) or value > 0:
        engine.wait_ge(semaphore, value)


def interleaved(peer, done):
    def upto(t):
        while peer is not None and done[0] < t:
            next(peer)
            done[0] += 1
    return upto


class Arena:

    def __init__(self, tensor, at=0):
        self.tensor, self.at = tensor, at

    def take(self, *dims, dt=F32):
        n = int(np.prod(dims))
        v = self.tensor[:, self.at:self.at + n]
        self.at += n
        if dt != F32:
            v = v.bitcast(dt)
        if len(dims) == 2:
            v = v.rearrange("p (a b) -> p a b", a=dims[0])
        elif len(dims) == 3:
            v = v.rearrange("p (a b c) -> p a b c", a=dims[0], b=dims[1])
        return v


def build(nc, i_, o_):
    with ExitStack() as ctx:
        ARENA = 53100
        arena = ctx.enter_context(nc.sbuf_tensor("arena", [P, ARENA], F32))
        psum = ctx.enter_context(nc.psum_tensor("psum", [P, 8, 512], F32))
        x2_dram = nc.dram_tensor("x2_scratch", (TOK, D), F32, kind="Internal").ap()
        hn_dram = nc.dram_tensor("hn_scratch", (TOK, D), F32, kind="Internal").ap()
        s8_dram = nc.dram_tensor("s8_scratch", (NS, HEADS, 2 * NKEY), F32, kind="Internal").ap()
        idx_dram = nc.dram_tensor("idx_scratch", (NS, TOPK, HEADS), U32, kind="Internal").ap()
        g_dram = nc.dram_tensor("g_scratch", (NS, TOPK, HEADS), F32, kind="Internal").ap()

        def sem(name):
            return ctx.enter_context(nc.semaphore(name))

        T = Arena(arena)
        cosT = T.take(SJ, SEG)
        sinT = T.take(SJ, SEG)
        s5_at = T.at
        rc = T.take(2, C)
        rs = T.take(2, C)
        rv = T.take(2, C)
        hb = T.take(3, 2, C)
        s5_end = T.at
        bT = T.take(2, QT, P)
        cT = T.take(2, SJ, 32)
        hT = T.take(KT, N)
        ga = T.take(KT, N)
        gb = T.take(KT, N)
        nffn = ga.rearrange("p a b -> p (a b)")[:, 0:D]
        uS = T.take(QT, N)
        xl = T.take(QT, N + CONV - 1)
        xc = T.take(QT, N)
        gy = T.take(QT, N)
        lru_at = T.at
        rT = T.take(QT, N)
        yS = T.take(QT, N)
        tok_at = T.at
        iT = T.take(QT, N)
        sT = T.take(QT, N)
        hl = T.take(QT, N)
        x_tok = Arena(arena, tok_at).take(3, D)
        assert tok_at + 3 * D <= T.at
        ring = T.take(RING, D)
        rstd = T.take(N)
        ident = T.take(P)
        ones = T.take(P)
        bd = T.take(QT, 2, P)
        nmix = T.take(KT)
        prm = T.take(40)
        mag = T.take(SJ)
        pre = T.take(2, SJ, NS)
        hS = T.take(2, SJ, NS)
        carr = T.take(2, SJ)
        mid = T.take(2)
        midt = T.take(2)
        lcar = T.take(QT)
        cSmp = T.take(QT, NS)
        sconv = T.take(QT, CONV - 1, NS)
        slru = T.take(QT, NS)
        dum = T.take(NS)
        convb, dskip, bglu = prm[:, 0:4], prm[:, 4:8], prm[:, 8:12]
        bgate, lam, sp4 = prm[:, 12:20], prm[:, 20:24], prm[:, 24:28]
        convw = prm[:, 28:40]
        convw3 = T.take(QT)
        ztmp = T.take(QT, 6)
        qT = T.take(2, N)
        kb = T.take(2, 2, NKEY)

        S = Arena(arena, s5_at)
        lre, lim, ldt, th = (S.take(SJ) for _ in range(4))
        e0, e1, e2, e3, e4, e5 = (S.take(SJ) for _ in range(6))
        fre, fim = S.take(SJ), S.take(SJ)
        ei = S.take(SJ, dt=I32)
        TA, TB = SEG // 16, 16
        NT = TA + TB
        tau = S.take(NT)
        angles = S.take(2, SJ, NT)
        q0, q1 = angles[:, 0], angles[:, 1]
        q2 = S.take(SJ, NT)
        sc = S.take(2, SJ, NT)
        assert S.at <= s5_end
        W = Arena(arena, lru_at)
        braw = W.take(2, SJ, 16)
        bp = W.take(2, SJ, 32)
        b0, b1 = W.take(SJ, 16), W.take(SJ, 16)
        s0 = W.take(2, SJ, NS)
        HJ = SJ // 4
        big, big2 = W.take(HJ, SEG), W.take(HJ, SEG)
        assert W.at <= lru_at + 5 * QT * N

        R = Arena(arena, T.at)
        uring = R.take(4, D)
        vring = R.take(8, D)
        hnc = R.take(2, D)
        acc = R.take(2, D)
        nfin = R.take(D)
        dg = R.take(2 * ONPE, P)
        idxn = R.take(2 * HEADS, TOPK, dt=U32)
        gn = R.take(2 * HEADS, TOPK)
        idxc = R.take(2 * HEADS * TOPK, dt=U32)
        gc = R.take(2 * HEADS * TOPK)
        dots_ = R.take(2, 4)
        ac = R.take(2, 4)
        wt = R.take(4, 4)
        ss2, rt2 = R.take(1), R.take(1)
        i8 = R.take(TOPK, dt=U32)
        g8 = R.take(TOPK)
        iS = R.take(HEADS, dt=U32)
        gS, accS, acS, wS = (R.take(HEADS) for _ in range(4))
        mk, mk2 = R.take(NS), R.take(NS)
        w8 = R.take(HEADS, NS)
        sS = R.take(4, NKEY)
        sS8 = R.take(2, NKEY)
        ss = R.take(3)
        iota = R.take(16)
        assert R.at <= ARENA, R.at
        K = Arena(arena, s5_at)
        sM = K.take(4, NKEY)
        cd = K.take(2, 256)
        cd2 = K.take(2, 256)
        oh = K.take(4, 256)
        sv = K.take(4, 16)
        ct, esh, en = K.take(2, 16), K.take(2, 16), K.take(2, 16)
        esum, ersum = K.take(2), K.take(2)
        si = K.take(4, 16, dt=U32)
        pos = K.take(2, 16, dt=U32)
        ab = K.take(2, 2, 16, dt=U32)
        iab = K.take(4, 16)
        assert K.at <= s5_end

        par_in = sem("par_in")
        bd_in = sem("bd_in")
        const_ok = sem("const_ok")
        cz = sem("cz")
        halo_ok = sem("halo_ok")
        set_a = sem("set_a")
        set_b = sem("set_b")
        bp_ok = sem("bp_ok")
        bt_mm = sem("bt_mm")
        x_in = sem("x_in")
        tok_in = sem("tok_in")
        nf_in = sem("nf_in")
        slot_in = [sem(f"slot_in{k}") for k in range(RING)]
        key_in = [sem(f"key_in{k}") for k in range(2)]
        sq_ok, ss_ok = sem("sq_ok"), sem("ss_ok")
        ms_ok, rt_ok = sem("ms_ok"), sem("rt_ok")
        hT_ok = sem("hT_ok")
        unit = sem("unit")
        evac = sem("evac")
        conv_ok = sem("conv_ok")
        tanh_ok = sem("tanh_ok")
        lru_ok = sem("lru_ok")
        bu_ok = sem("bu_ok")
        bu_read = sem("bu_read")
        h_ok = sem("h_ok")
        y_mm = sem("y_mm")
        y_ok = sem("y_ok")
        z_ok = sem("z_ok")
        smp_mm, smp_ok = sem("smp_mm"), sem("smp_ok")
        a_ok = sem("a_ok")
        mix_ok = sem("mix_ok")
        x2_ok = sem("x2_ok")
        x2_out = sem("x2_out")
        sq2_ok, ms2_ok, rt2_ok = sem("sq2_ok"), sem("ms2_ok"), sem("rt2_ok")
        hn_ok = sem("hn_ok")
        hn_out = sem("hn_out")
        tr_ok, tr_ev = sem("tr_ok"), sem("tr_ev")
        s_mm, s_ev = sem("s_mm"), sem("s_ev")
        cs_ok, exp_ok = sem("cs_ok"), sem("exp_ok")
        idx_ok = sem("idx_ok")
        st_out = sem("st_out")
        pool_at = sem("pool_at")
        dve_at = sem("dve_at")
        act_at = sem("act_at")
        sp_at = sem("sp_at")
        u_in = [sem(f"u_in{k}") for k in range(4)]
        v_in = [sem(f"v_in{k}") for k in range(8)]
        u_used = sem("u_used")
        v_pe = sem("v_pe")
        v_dve = sem("v_dve")
        gelu_ok, w_ok, dg_ok = sem("gelu_ok"), sem("w_ok"), sem("dg_ok")
        hnc_in, acc_in = [sem(f"hnc_in{k}") for k in range(2)], [sem(f"acc_in{k}") for k in range(2)]
        pv_ok = sem("pv_ok")
        add_ok = sem("add_ok")
        sum_ok = sem("sum_ok")
        fm_ok, fr_ok = sem("fm_ok"), sem("fr_ok")
        yo_ok = sem("yo_ok")
        y_out = sem("y_out")
        i8_ok, sc_out, sc_in = sem("i8_ok"), sem("sc_out"), sem("sc_in")
        hnS_in = sem("hnS_in")
        s8_out, s8_in = sem("s8_out"), sem("s8_in")
        w8_ok = sem("w8_ok")

        PB = [psum[:, 0, :], psum[:, 1, :]]
        SB = [psum[:, 2, :], psum[:, 3, :]]
        YB = [psum[:, 4, :], psum[:, 5, :]]
        OUTB = [PB, YB, SB]
        MIXB = [SB, YB]
        PV = psum[:, 6:8, :]
        PVf = PV.rearrange("p a b -> p (a b)")

        def flat(v):
            return v.rearrange("p a b -> p (a b)")

        def rows_of(last):
            return [(0, P, 0), (1, P, P)] + ([(2, NS, C)] if last else [])

        block = ctx.enter_context(nc.Block())

        @block.sync
        def _(sp):
            sp.dma_start(hT[:, :, 0:C], i_["xT"][:, :, 0:C]).then_inc(x_in, 16)
            weights = [i_["w_in"][m] for m in range(28)] + [i_["w_glu"][m] for m in range(4)] \
                + [i_["w_ab"][m] for m in range(8)] + [i_["w_out"][m] for m in range(8)] \
                + [i_["w_q"][m] for m in range(16)]

            def load_weights(l):
                width = weights[l].shape[1]
                sp.dma_start(ring[:, l % RING, 0:width], weights[l]).then_inc(slot_in[l % RING], 16)

            for name, dst in (("lam_re", lre), ("lam_im", lim), ("prm", prm), ("nmix", nmix), ("b_raw", braw),
                              ("c_raw", cT), ("s5_0", s0), ("sconv", sconv), ("slru", slru), ("convw3", convw3)):
                sp.dma_start(dst, i_[name]).then_inc(par_in, 16)
            for g2 in range(2):
                sp.dma_start(ldt[64 * g2:64 * g2 + 64, :], i_["log_dt"][g2].partition_broadcast(64)).then_inc(par_in, 16)
            for l in range(RING):
                load_weights(l)
            sp.dma_start(bd, i_["lru_bd"]).then_inc(bd_in, 16)
            sp.dma_start(nfin, i_["norm_final"].partition_broadcast(P)).then_inc(nf_in, 16)

            def wait(semaphore, value):
                sp.wait_ge(semaphore, value)
                sp.sem_inc(sp_at, 1)

            def load_acc(c):
                for t in range(2):
                    sp.dma_start(acc[:, t], x2_dram[bass.ds(c * C + t * P, P), :]).then_inc(acc_in[t], 16)

            def store_y(c, t):
                wait(yo_ok, 2 * c + t + 1)
                sp.dma_start(o_["y_prompt"][bass.ds(c * C + t * P, P), :], acc[:, t]).then_inc(y_out, 16)

            def chunk(c, cp, last):
                if cp is not None:
                    load_acc(cp)
                for l in range(RING, SLOTS):
                    if l == 52:
                        if cp is not None:
                            store_y(cp, 0)
                        for t, rn, r0 in rows_of(last):
                            wait(x2_ok, 4 * c + 2 * t + 2)
                            sp.dma_start(x2_dram[bass.ds(c * C + r0, rn), :], x_tok[0:rn, t, :]).then_inc(x2_out, 16)
                        if not last:
                            n = columns(c + 1)
                            sp.dma_start(hT[:, :, 0:n], i_["xT"][:, :, bass.ds((c + 1) * C, n)]).then_inc(x_in, 16)
                        for t, rn, r0 in rows_of(last):
                            wait(hn_ok, 2 * c + t + 1)
                            sp.dma_start(hn_dram[bass.ds(c * C + r0, rn), :], x_tok[0:rn, t, :]).then_inc(hn_out, 16)
                    if l == 48:
                        sp.wait_ge(mix_ok, KT * (c + 1))
                        sp.dma_start(nffn, i_["norm_ffn"].partition_broadcast(P)).then_inc(nf_in, 16)
                    if l >= 48 and l % 2 == 0:
                        h = (l - 48) // 2
                        need(sp, s_mm, HEADS * c + h - 1)
                        sp.dma_start(kb[:, h % 2], i_["keys"][:, 2 * h:2 * h + 2, :]).then_inc(key_in[h % 2], 16)
                    sp.wait_ge(unit, UNITS * c + slot_unit(l - RING) + 1)
                    load_weights(l)
                    if l == 40:
                        wait(lru_ok, QT * (c + 1))
                        for t, rn, r0 in rows_of(last):
                            sp.dma_start(x_tok[0:rn, t, :], i_["x_tok"][bass.ds(c * C + r0, rn), :]).then_inc(tok_in, 16)
                if not last:
                    for l in range(RING):
                        sp.wait_ge(unit, UNITS * c + slot_unit(SLOTS - RING + l) + 1)
                        load_weights(l)
                wait(x2_out, 16 * (2 * (c + 1) + (1 if last else 0)))
                if cp is not None:
                    store_y(cp, 1)
                    wait(y_out, 32 * (cp + 1))

            chunk(0, None, False)
            with sp.Fori(0, CH - 2) as cp:
                chunk(cp + 1, cp, False)
            chunk(CH - 1, CH - 2, True)
            sp.dma_start(o_["s5_s"], hS).then_inc(st_out, 16)
            sp.dma_start(o_["s5_p"], carr).then_inc(st_out, 16)
            sp.dma_start(o_["lru_p"], lcar).then_inc(st_out, 16)
            sp.dma_start(o_["lru_s"], slru).then_inc(st_out, 16)
            sp.dma_start(o_["conv_p"], xl[:, :, C:C + 3]).then_inc(st_out, 16)
            sp.dma_start(o_["conv_s"][:, :, 0:2, :], sconv[:, :, 1:3, :]).then_inc(st_out, 16)
            sp.dma_start(o_["conv_s"][:, :, 2, :], xl[:, :, 3 + C:3 + N]).then_inc(st_out, 16)
            load_acc(CH - 1)
            sp.wait_ge(i8_ok, 1)
            for t in range(NS):
                rows = slice(HEADS * t, HEADS * t + HEADS)
                sp.dma_start(idx_dram[t].rearrange("k h -> h k"), i8[rows], allow_slow_non_contiguous=True).then_inc(sc_out, 16)
                sp.dma_start(g_dram[t].rearrange("k h -> h k"), g8[rows], allow_slow_non_contiguous=True).then_inc(sc_out, 16)
            sp.wait_ge(sc_out, 32 * NS)
            sp.dma_start(iS, idx_dram.rearrange("t k h -> (t k) h")).then_inc(sc_in, 16)
            sp.dma_start(gS, g_dram.rearrange("t k h -> (t k) h")).then_inc(sc_in, 16)
            sp.wait_ge(hn_out, 16 * (2 * CH + 1))
            store_y(CH - 1, 0)
            sp.wait_ge(y_out, 16 * (2 * CH - 1))
            sp.dma_start(acc[0:NS, 0], x2_dram[SEQ:TOK, :]).then_inc(acc_in[0], 16)
            sp.wait_ge(u_used, 4 * (BC * CH - BT) + 4)
            for t in range(NS):
                sp.dma_start(hnc[16 * t:16 * t + 16, 0], hn_dram[SEQ + t].partition_broadcast(16)).then_inc(hnS_in, 16)
            store_y(CH - 1, 1)
            sp.wait_ge(yo_ok, TILES + 1)
            sp.dma_start(o_["y_sample"], acc[0:NS, 0]).then_inc(y_out, 16)
            sp.wait_ge(y_out, 16 * (TILES + 1))
            sp.wait_ge(st_out, 16 * 7)

        @block.gpsimd
        def _(pool):
            pool.memset(ident, 0.0).then_inc(cz, 1)
            pool.memset(ones, 1.0).then_inc(const_ok, 1)
            pool.memset(xl[:, :, 0:CONV - 1], 0.0).then_inc(halo_ok, 1)
            pool.wait_ge(cz, 1)
            pool.affine_select(out=ident, in_=ident, compare_op=ALU.not_equal, fill=1.0, base=0,
                               pattern=[[-1, P]], channel_multiplier=1).then_inc(const_ok, 1)
            for out, pattern, base, mult in ((tau[:, 0:TA], [[TB, TA]], 0, 0), (tau[:, TA:NT], [[1, TB]], 1, 0),
                                             (iota, [[1, 16]], 0, 0), (mk, [[-16, NS]], 0, 1)):
                pool.iota(out, pattern, base=base, channel_multiplier=mult,
                          allow_small_or_imprecise_dtypes=True).then_inc(const_ok, 1)

            def gathers(c):
                pool.wait_ge(idx_ok, c + 1)
                pool.sem_inc(pool_at, 1)
                for n in range(BC + 1):
                    for k in range(4):
                        if n < BC:
                            pool.wait_ge(u_used, 4 * (BC * c + n) + k + 1)
                            pool.sem_inc(pool_at, 1)
                            pool.indirect_dma_start(uring[:, k, :], None, i_["u"],
                                                    bass.IndirectOffsetOnAxis(idxc[:, 4 * n + k:4 * n + k + 1], 0)).then_inc(u_in[k], 16)
                        if n > 0:
                            m = n - 1
                            if k in (0, ONPE):
                                pool.wait_ge(v_pe if k < ONPE else v_dve, BC * c + m + 1)
                                pool.sem_inc(pool_at, 1)
                            s = 4 * (m % 2) + k
                            pool.indirect_dma_start(vring[:, s, :], None, i_["v"],
                                                    bass.IndirectOffsetOnAxis(idxc[:, 4 * m + k:4 * m + k + 1], 0)).then_inc(v_in[s], 16)

            with pool.Fori(0, CH - 1) as c:
                gathers(c)
            gathers(CH - 1)
            pool.wait_ge(sc_in, 32)
            NB = BC * CH
            for h in range(HEADS):
                pool.wait_ge(u_used, 4 * NB + h + 1)
                pool.indirect_dma_start(uring[:, h % 4, :], None, i_["u"],
                                        bass.IndirectOffsetOnAxis(iS[:, h:h + 1], 0)).then_inc(u_in[h % 4], 16)
            pool.wait_ge(v_pe, NB + 2)
            pool.wait_ge(v_dve, NB + 2)
            for h in range(HEADS):
                pool.indirect_dma_start(vring[:, h, :], None, i_["v"],
                                        bass.IndirectOffsetOnAxis(iS[:, h:h + 1], 0)).then_inc(v_in[h], 16)

        @block.scalar
        def _(act):
            def af(out, in_, f, **kw):
                return nc.scalar.activation(out, in_, f, **kw)

            def norm(c, n):
                act.wait_ge(x_in, 16 * (c + 1))
                need(act, hn_ok, 2 * c)
                af(ga[:, :, 0:n], hT[:, :, 0:n], ACT.Square).then_inc(sq_ok, 1)
                act.wait_ge(ms_ok, c + 1)
                af(rstd[:, 0:n], rstd[:, 0:n], ACT.Sqrt).then_inc(rt_ok, 1)

            def batches(c):
                for s in range(BS):
                    if s == 2:
                        load_hn(c, 1)
                    if s < BC:
                        act.wait_ge(u_used, 4 * (BC * c + s) + 8)
                        af(ac[:, s % 2, :], dots_[:, s % 2, :], ACT.Gelu_apprx_tanh).then_inc(gelu_ok, 1)
                    if 1 <= s <= BC:
                        b = s - 1
                        act.wait_ge(w_ok, BC * c + b + 1)
                        act.wait_ge(v_pe, BC * c + b + 1)
                        for k in range(ONPE):
                            ins = af(dg[:, ONPE * (b % 2) + k, :], ident, ACT.Copy, scale=wt[:, b % 4, k:k + 1])
                        ins.then_inc(dg_ok, 1)
                    for t in range(2):
                        if s == BT * (t + 1) + 2:
                            squares(2 * c + t, t, P)
                        elif s == BT * (t + 1) + 3:
                            root(2 * c + t, P)
                    yield

            def load_hn(c, t):
                act.wait_ge(hn_out, hn_stored(c))
                act.sem_inc(act_at, 1)
                act.dma_start(hnc[:, t], hn_dram[bass.ds(c * C + P * t, P), :]).then_inc(hnc_in[t], 16)

            def squares(i, t, rows):
                act.wait_ge(add_ok, i + 1)
                af(PVf[0:rows], acc[0:rows, t], ACT.Square, accum_out=ss2[0:rows]).then_inc(sum_ok, 1)

            def root(i, rows):
                act.wait_ge(fm_ok, i + 1)
                af(rt2[0:rows], ss2[0:rows], ACT.Sqrt).then_inc(fr_ok, 1)

            def soft(n, rows, tiles):
                act.wait_ge(cs_ok, n + 1)
                for t in range(tiles):
                    ins = af(en[0:rows, t], esh[0:rows, t], ACT.Exp, accum_out=esum[0:rows, t:t + 1])
                ins.then_inc(exp_ok, 1)

            def chunk(c, cp, last):
                n = N if last else C
                upto = interleaved(None if cp is None else batches(cp), [0])
                act.wait_ge(halo_ok, c + 1)
                for q in range(QT):
                    upto(q // 2)
                    act.wait_ge(unit, UNITS * c + U_XL + q + 1)
                    af(xl[:, q, CONV - 1:CONV - 1 + n], PB[q % 2][:, 0:n], ACT.Copy).then_inc(evac, 1)
                for q in range(QT):
                    upto((U_U + q) // 2)
                    act.wait_ge(unit, UNITS * c + U_U + q + 1)
                    af(uS[:, q, 0:n], PB[q % 2][:, 0:n], ACT.Copy).then_inc(evac, 1)
                for q in range(QT):
                    upto((U_YL + q) // 2)
                    act.wait_ge(unit, UNITS * c + U_YL + q + 1)
                    af(gy[:, q, 0:n], PB[q % 2][:, 0:n], ACT.Gelu_apprx_tanh).then_inc(evac, 1)
                upto(AT_GATE)
                if not (isinstance(c, int) and c == 0):
                    act.wait_ge(hn_out, 32 * c)
                need(act, x2_out, 32 * c)
                for q in range(QT):
                    for s, dst in ((0, rT), (1, iT)):
                        act.wait_ge(unit, UNITS * c + U_GATE + 2 * q + s + 1)
                        af(dst[:, q, 0:n], PB[s][:, 0:n], ACT.Sigmoid,
                           bias=bgate[:, 4 * s + q:4 * s + q + 1]).then_inc(evac, 1)
                act.drain()
                for q in range(QT):
                    af(rT[:, q, 0:n], rT[:, q, 0:n], ACT.Tanh, scale=sp4[:, q:q + 1])
                act.drain()
                af(sT[:, :, 0:n], rT[:, :, 0:n], ACT.Sqrt).then_inc(tanh_ok, 1)
                for m in range(2 * KT):
                    upto(AT_S5 + m)
                    act.wait_ge(unit, UNITS * c + U_GA + m + 1)
                    dst = (ga if m < KT else gb)[:, m % KT, 0:n]
                    af(dst, PB[m % 2][:, 0:n], ACT.Sigmoid).then_inc(evac, 1)
                for q in range(QT):
                    upto(at_y(QT - 1))
                    act.wait_ge(y_ok, QT * c + q + 1)
                    af(yS[:, q, 0:C], yS[:, q, 0:C], ACT.Gelu_apprx_tanh).then_inc(z_ok, 1)
                if last:
                    act.wait_ge(smp_ok, 2)
                    af(yS[:, :, C:N], yS[:, :, C:N], ACT.Gelu_apprx_tanh).then_inc(z_ok, 1)
                upto(AT_GLU)
                for q in range(QT):
                    act.wait_ge(unit, UNITS * c + U_GLU + q + 1)
                    af(rT[:, q, 0:n], PB[q % 2][:, 0:n], ACT.Sigmoid, bias=bglu[:, q:q + 1]).then_inc(evac, 1)
                upto(AT_HN)
                for t, rn, r0 in rows_of(last):
                    act.wait_ge(x2_ok, 4 * c + 2 * t + 2)
                    af(gb[0:rn].rearrange("p a b -> p (a b)")[:, 0:D], x_tok[0:rn, t, :], ACT.Square,
                       accum_out=ss[0:rn, t:t + 1])
                    act.drain()
                act.sem_inc(sq2_ok, 1)
                act.wait_ge(ms2_ok, c + 1)
                af(ss[:, 0:2], ss[:, 0:2], ACT.Sqrt)
                if last:
                    af(ss[0:NS, 2:3], ss[0:NS, 2:3], ACT.Sqrt)
                act.drain()
                act.sem_inc(rt2_ok, 1)
                upto(AT_TR)
                act.wait_ge(tr_ok, c + 1)
                for t, banks in ((0, psum[:, 2:4]), (1, psum[:, 4:6])):
                    af(gb[:, :, P * t:P * t + P], banks.rearrange("p a (k b) -> p (a k) b", b=P), ACT.Copy)
                if last:
                    af(gb[:, :, C:N], psum[:, 0, 0:KT * NS].rearrange("p (k b) -> p k b", b=NS), ACT.Copy)
                act.drain()
                act.sem_inc(tr_ev, 1)
                for h in range(HEADS):
                    upto(at_q(h))
                    for s in range(2):
                        act.wait_ge(unit, UNITS * c + U_Q + 2 * h + s + 1)
                        af(qT[:, s, 0:n], PB[s][:, 0:n], ACT.Copy).then_inc(evac, 1)
                    act.wait_ge(s_mm, HEADS * c + h + 1)
                    af(flat(sS), YB[h % 2], ACT.Copy)
                    if last:
                        if h:
                            act.wait_ge(s8_out, 16 * h)
                        af(flat(sS8[0:NS]), SB[h % 2][0:NS, 0:2 * NKEY], ACT.Copy)
                    act.drain()
                    act.sem_inc(s_ev, 1)
                    if last:
                        act.dma_start(s8_dram[:, h, :], flat(sS8[0:NS])).then_inc(s8_out, 16)
                    upto(at_q(h) + 1)
                    soft(HEADS * c + h, P, 2)
                if last:
                    act.wait_ge(s8_out, 16 * HEADS)
                    act.dma_start(flat(sS[0:NS * HEADS, 0:2]), s8_dram.rearrange("t h k -> (t h) k")).then_inc(s8_in, 16)
                    upto(AT_NORM)
                    soft(HEADS * CH, NS * HEADS, 1)
                upto(AT_NORM)
                if cp is not None:
                    act.wait_ge(u_used, 4 * (BC * cp + BT) + 4)
                load_hn(c, 0)
                if not last:
                    norm(c + 1, columns(c + 1))
                upto(BS)

            act.sem_inc(sum_ok, 1)
            norm(0, C)
            act.wait_ge(set_a, 1)
            af(e1, e0, ACT.Tanh)
            af(ztmp[:, :, 1], ztmp[:, :, 0], ACT.Exp)
            act.drain()
            act.wait_ge(set_a, 2)
            af(sc, angles, ACT.Sin).then_inc(set_b, 1)
            act.wait_ge(const_ok, 6)
            chunk(0, None, False)
            with act.Fori(0, CH - 2) as cp:
                chunk(cp + 1, cp, False)
            chunk(CH - 1, CH - 2, True)
            for _ in batches(CH - 1):
                pass
            act.wait_ge(u_used, 4 * BC * CH + HEADS + 4)
            af(acS, accS, ACT.Gelu_apprx_tanh).then_inc(gelu_ok, 1)
            squares(TILES, 0, NS)
            root(TILES, NS)

        @block.vector
        def _(dve):
            V = nc.vector

            def tt(out, a, b, op):
                return V.tensor_tensor(out, a, b, op)

            def ts(out, a, s1, s2=None, op0=ALU.mult, op1=ALU.add):
                if s2 is None:
                    return V.tensor_scalar(out, a, s1, None, op0)
                return V.tensor_scalar(out, a, s1, s2, op0, op1)

            def stt(out, a, s1, b, op0=ALU.mult, op1=ALU.add):
                return V.scalar_tensor_tensor(out=out, in0=a, scalar=s1, in1=b, op0=op0, op1=op1)

            def chain(*steps):
                for f in steps:
                    f()
                    dve.drain()

            def norm(c, n):
                dve.wait_ge(ss_ok, c + 1)
                ts(rstd[:, 0:n], YB[0][:, 0:n], 1.0 / D, EPS).then_inc(ms_ok, 1)
                dve.wait_ge(rt_ok, c + 1)
                V.reciprocal(rstd[:, 0:n], rstd[:, 0:n])
                dve.drain()
                for k in range(KT):
                    stt(hT[:, k, 0:n], hT[:, k, 0:n], nmix[:, k:k + 1], rstd[:, 0:n], ALU.mult, ALU.mult).then_inc(hT_ok, 1)

            dve.memset(carr, 0.0)
            dve.memset(lcar, 0.0)
            dve.memset(bp, 0.0)
            dve.wait_ge(par_in, 16 * 12)
            norm(0, C)
            dve.wait_ge(const_ok, 6)
            ts(mk2, mk, 0.0, None, ALU.is_ge)
            dve.drain()
            ts(mk, mk, 16.0, None, ALU.is_lt)
            dve.drain()
            tt(mk2, mk2, mk, ALU.mult)
            dve.drain()
            dve.sem_inc(u_used, 4)
            dve.sem_inc(v_dve, 2)
            LN2H, LN2L = 0.693359375, -2.12194440e-4
            MAGIC = 12582912.0
            chain(
                lambda: ts(e0, ldt, -87.0, 88.0, ALU.max, ALU.min),
                lambda: ts(e1, e0, 1.4426950408889634, MAGIC, ALU.mult, ALU.add),
                lambda: ts(e1, e1, MAGIC, None, ALU.subtract),
                lambda: V.scalar_tensor_tensor(out=e2, in0=e1, scalar=-LN2H, in1=e0, op0=ALU.mult, op1=ALU.add),
                lambda: V.scalar_tensor_tensor(out=e2, in0=e1, scalar=-LN2L, in1=e2, op0=ALU.mult, op1=ALU.add),
                lambda: ts(e3, e2, 1.0 / 5040, 1.0 / 720),
            )
            for coef in (1.0 / 120, 1.0 / 24, 1.0 / 6, 0.5, 1.0, 1.0):
                chain(lambda: tt(e3, e3, e2, ALU.mult), lambda: ts(e3, e3, 1.0, coef))
            chain(
                lambda: ts(e1, e1, 127.0, 8388608.0, ALU.add, ALU.mult),
                lambda: V.tensor_copy(ei, e1),
                lambda: tt(e5, e3, ei.bitcast(F32), ALU.mult),
                lambda: tt(th, lim, e5, ALU.mult),
                lambda: tt(e0, lre, e5, ALU.mult),
                lambda: ts(e0, e0, -0.5),
            )
            zl = [ztmp[:, :, k] for k in range(6)]
            chain(
                lambda: ts(zl[2], lam, -1.0),
                lambda: tt(zl[3], lam, zl[2], ALU.min),
                lambda: V.tensor_copy(zl[0], zl[3]),
                lambda: ts(zl[5], zl[2], 0.0, None, ALU.max),
            )
            dve.sem_inc(set_a, 1)
            def bt3(a):
                return a.unsqueeze(2).to_broadcast([P, SJ, NT])
            taub = tau.unsqueeze(1).to_broadcast([P, SJ, NT])
            C1, C2 = 6.28125, 0.0019350051879882812
            C3 = 6.283185307179586 - C1 - C2
            chain(
                lambda: ts(e2, th, 4097.0),
                lambda: tt(e3, e2, th, ALU.subtract),
                lambda: tt(e3, e2, e3, ALU.subtract),
                lambda: tt(e4, th, e3, ALU.subtract),
                lambda: tt(q0, bt3(e3), taub, ALU.mult),
                lambda: tt(q1, bt3(e4), taub, ALU.mult),
                lambda: tt(q2, q0, q1, ALU.add),
                lambda: ts(q2, q2, 1.0 / 6.283185307179586, MAGIC),
                lambda: ts(q2, q2, MAGIC, None, ALU.subtract),
                lambda: V.scalar_tensor_tensor(out=q0, in0=q2, scalar=-C1, in1=q0, op0=ALU.mult, op1=ALU.add),
                lambda: V.scalar_tensor_tensor(out=q0, in0=q2, scalar=-C2, in1=q0, op0=ALU.mult, op1=ALU.add),
                lambda: V.scalar_tensor_tensor(out=q0, in0=q2, scalar=-C3, in1=q0, op0=ALU.mult, op1=ALU.add),
                lambda: tt(q0, q0, q1, ALU.add),
                lambda: ts(q1, q0, 1.5707963267948966, None, ALU.add),
                lambda: ts(q2, q1, 3.1415925, -6.283185307179586, ALU.is_gt, ALU.mult),
                lambda: tt(q1, q1, q2, ALU.add),
                lambda: ts(q0, q0, -3.1415925, 3.1415925, ALU.max, ALU.min),
                lambda: ts(q1, q1, -3.1415925, 3.1415925, ALU.max, ALU.min),
            )
            dve.sem_inc(set_a, 1)
            dve.wait_ge(set_b, 1)
            chain(
                lambda: ts(e2, e1, 1.0, None, ALU.add),
                lambda: V.reciprocal(e2, e2),
                lambda: ts(mag, e2, 2.0, -1.0),
            )
            chain(
                lambda: ts(zl[2], zl[1], 2.0, None, ALU.add),
                lambda: V.reciprocal(zl[2], zl[2]),
                lambda: tt(zl[2], zl[1], zl[2], ALU.mult),
                lambda: tt(zl[3], zl[2], zl[2], ALU.mult),
                lambda: ts(zl[4], zl[3], 1.0 / 15, 1.0 / 13),
            )
            for m in (11, 9, 7, 5, 3, 1):
                chain(lambda: tt(zl[4], zl[4], zl[3], ALU.mult), lambda: ts(zl[4], zl[4], 1.0, 1.0 / m))
            chain(
                lambda: tt(zl[4], zl[4], zl[2], ALU.mult),
                lambda: ts(zl[4], zl[4], 2.0),
                lambda: tt(zl[4], zl[4], zl[5], ALU.add),
                lambda: ts(sp4, zl[4], 4.0),
            )
            a_re, a_im, den = e0, e1, e2
            chain(
                lambda: tt(a_re, mag, sc[:, 1, :, TA], ALU.mult),
                lambda: tt(a_im, mag, sc[:, 0, :, TA], ALU.mult),
                lambda: tt(e3, lre, lre, ALU.mult),
                lambda: tt(e4, lim, lim, ALU.mult),
                lambda: tt(den, e3, e4, ALU.add),
                lambda: V.reciprocal(den, den),
                lambda: ts(e5, a_re, 1.0, None, ALU.subtract),
                lambda: tt(e3, e5, lre, ALU.mult),
                lambda: tt(e4, a_im, lim, ALU.mult),
                lambda: tt(e3, e3, e4, ALU.add),
                lambda: tt(fre, e3, den, ALU.mult),
                lambda: tt(e3, a_im, lre, ALU.mult),
                lambda: tt(e4, e5, lim, ALU.mult),
                lambda: tt(e3, e3, e4, ALU.subtract),
                lambda: tt(fim, e3, den, ALU.mult),
            )
            def over(a, n):
                return a.unsqueeze(2).to_broadcast([P, SJ, n])
            for part, (x, y, op) in enumerate(((0, 1, ALU.subtract), (1, 0, ALU.add))):
                tt(b0, over(fre, 16), braw[:, x], ALU.mult)
                tt(b1, over(fim, 16), braw[:, y], ALU.mult)
                dve.drain()
                for g2 in range(2):
                    r = slice(64 * g2, 64 * g2 + 64)
                    tt(bp[r, part, :, 16 * g2:16 * g2 + 16], b0[r], b1[r], op)
                dve.drain()
            ts(cT[:, 1], cT[:, 1], -1.0)
            dve.drain()
            dve.sem_inc(bp_ok, 1)
            for part, (x, y, op) in enumerate(((0, 1, ALU.subtract), (1, 0, ALU.add))):
                w0, w1 = b0[:, :, 0:NS], b1[:, :, 0:NS]
                tt(w0, over(a_re, NS), s0[:, x], ALU.mult)
                tt(w1, over(a_im, NS), s0[:, y], ALU.mult)
                dve.drain()
                tt(pre[:, part], w0, w1, op)
                dve.drain()
            for q in range(QT):
                for k in range(CONV - 1):
                    if k == 0:
                        ts(cSmp[:, q], sconv[:, q, 0], convw[:, q:q + 1], convb[:, q:q + 1])
                    else:
                        V.scalar_tensor_tensor(out=cSmp[:, q], in0=sconv[:, q, k], scalar=convw[:, 4 * k + q:4 * k + q + 1],
                                               in1=cSmp[:, q], op0=ALU.mult, op1=ALU.add)
                    dve.drain()
            for quarter in range(SJ // HJ):
                js = slice(HJ * quarter, HJ * quarter + HJ)

                def small(part, axis, js=js):
                    v = sc[:, part, js, 0:TA] if axis == 0 else sc[:, part, js, TA:NT]
                    return v.unsqueeze(3 if axis == 0 else 2).to_broadcast([P, HJ, TA, TB])
                b4 = [x.rearrange("p j (a b) -> p j a b", a=TA) for x in (big, big2)]
                for dst, (p0, p1), (p2, p3), op in ((cosT, (1, 1), (0, 0), ALU.subtract),
                                                    (sinT, (0, 1), (1, 0), ALU.add)):
                    tt(b4[0], small(p0, 0), small(p1, 1), ALU.mult)
                    tt(b4[1], small(p2, 0), small(p3, 1), ALU.mult)
                    dve.drain()
                    tt(dst[:, js], big, big2, op)
                    dve.drain()
            dve.wait_ge(bt_mm, 1)
            for part in range(2):
                V.tensor_copy(flat(bT[:, part]), SB[part])
            dve.drain()
            dve.sem_inc(bp_ok, 1)

            def conv(c, q, last):
                n = N if last else C
                dve.wait_ge(evac, EVACS * c + U_XL + q + 1)
                ts(xc[:, q, 0:C], xl[:, q, 0:C], convw[:, q:q + 1], convb[:, q:q + 1])
                dve.drain()
                for k in range(1, CONV):
                    w = convw[:, 4 * k + q:4 * k + q + 1] if k < CONV - 1 else convw3[:, q:q + 1]
                    stt(xc[:, q, 0:C], xl[:, q, k:k + C], w, xc[:, q, 0:C])
                    dve.drain()
                if last:
                    stt(xc[:, q, C:N], xl[:, q, 3 + C:3 + N], convw3[:, q:q + 1], cSmp[:, q])
                    dve.drain()
                dve.sem_inc(conv_ok, 1)

            def by_seg(v):
                return v.rearrange("p a (s t) -> p (a s) t", t=SEG)

            def s5(c, j):
                bu = SB[j % 2].rearrange("p (a t) -> p a t", t=SEG)
                h = hb[:, j % 3]
                cos4 = cosT[:, j].unsqueeze(1).to_broadcast([P, 4, SEG])
                sin4 = sinT[:, j].unsqueeze(1).to_broadcast([P, 4, SEG])
                cosE, sinE = cosT[:, j, SEG - 1:SEG], sinT[:, j, SEG - 1:SEG]
                m = mag[:, j:j + 1].to_broadcast([P, SEG])
                dve.wait_ge(bu_ok, SJ * c + j + 1)
                tt(by_seg(rc), bu, cos4, ALU.mult)
                tt(by_seg(rs), bu, sin4, ALU.mult).then_inc(bu_read, 1)
                dve.drain()
                tt(rv[:, 0], rc[:, 0], rs[:, 1], ALU.add)
                tt(rv[:, 1], rc[:, 1], rs[:, 0], ALU.subtract)
                dve.drain()
                for part in range(2):
                    V.tensor_tensor_scan(rv[:, part, 0:SEG], m, rv[:, part, 0:SEG], carr[:, part, j:j + 1], ALU.mult, ALU.add)
                dve.drain()
                g = [rv[:, part, SEG - 1:SEG] for part in range(2)]
                ts(midt[:, 0:1], g[1], sinE)
                ts(midt[:, 1:2], g[0], sinE)
                dve.drain()
                stt(mid[:, 0:1], g[0], cosE, midt[:, 0:1], ALU.mult, ALU.subtract)
                stt(mid[:, 1:2], g[1], cosE, midt[:, 1:2], ALU.mult, ALU.add)
                dve.drain()
                for part in range(2):
                    V.tensor_tensor_scan(rv[:, part, SEG:C], m, rv[:, part, SEG:C], mid[:, part:part + 1], ALU.mult, ALU.add)
                dve.drain()
                tt(by_seg(rc), by_seg(rv), cos4, ALU.mult)
                tt(by_seg(rs), by_seg(rv), sin4, ALU.mult)
                dve.drain()
                if j >= 3:
                    dve.wait_ge(y_mm, SJ * c + j - 2)
                tt(h[:, 0], rc[:, 0], rs[:, 1], ALU.subtract)
                tt(h[:, 1], rc[:, 1], rs[:, 0], ALU.add)
                dve.drain()
                V.tensor_copy(carr[:, :, j:j + 1], h[:, :, C - 1:C])
                dve.drain()
                dve.sem_inc(h_ok, 1)

            def lru(c, q, last):
                n = N if last else C
                if q == 0:
                    dve.wait_ge(tanh_ok, c + 1)
                r, s, i, h = rT[:, q, 0:n], sT[:, q, 0:n], iT[:, q, 0:n], hl[:, q, 0:n]
                ts(r, r, 1.0, None, ALU.add)
                tt(i, i, xc[:, q, 0:n], ALU.mult)
                dve.drain()
                V.reciprocal(r, r)
                dve.drain()
                tt(s, s, r, ALU.mult)
                dve.drain()
                ts(r, r, 2.0, -1.0)
                stt(i, i, 2.0, s, ALU.mult, ALU.mult)
                dve.drain()
                V.tensor_tensor_scan(h[:, 0:C], r[:, 0:C], i[:, 0:C], lcar[:, q:q + 1], ALU.mult, ALU.add)
                if last:
                    tt(dum, r[:, C:N], slru[:, q], ALU.mult)
                    dve.drain()
                    tt(h[:, C:N], dum, i[:, C:N], ALU.add)
                dve.drain()
                V.tensor_copy(lcar[:, q:q + 1], h[:, C - 1:C])
                if last:
                    V.tensor_copy(slru[:, q], h[:, C:N])
                tt(gy[:, q, 0:n], gy[:, q, 0:n], h, ALU.mult)
                dve.drain()
                dve.sem_inc(lru_ok, 1)

            def y_tile(c, q):
                dve.wait_ge(y_mm, SJ * c + 4 * q + 4)
                stt(yS[:, q, 0:C], uS[:, q, 0:C], dskip[:, q:q + 1], YB[q % 2][:, 0:C]).then_inc(y_ok, 1)

            def topk(n, rows, tiles, weights, experts):
                K2 = 2 * tiles
                src, M, O = sS[0:rows, 0:K2], sM[0:rows, 0:K2], oh[0:rows, 0:K2]
                SV, SI, IA = sv[0:rows, 0:K2], si[0:rows, 0:K2], iab[0:rows, 0:K2]
                X1, X2, CT, PO = cd[0:rows, 0:tiles], cd2[0:rows, 0:tiles], ct[0:rows, 0:tiles], pos[0:rows, 0:tiles]
                A, EN, RS = ab[0:rows, 0:tiles], en[0:rows, 0:tiles], ersum[0:rows, 0:tiles]
                best, rest = slice(0, 8), slice(8, 16)
                for k in range(K2):
                    V.max(SV[:, k, best], src[:, k])
                dve.drain()
                for k in range(K2):
                    V.max_index(SI[:, k, best], SV[:, k, best], src[:, k])
                    V.match_replace(M[:, k], SV[:, k, best], src[:, k], NEG)
                dve.drain()
                for k in range(K2):
                    V.max(SV[:, k, rest], M[:, k])
                dve.drain()
                for k in range(K2):
                    V.max_index(SI[:, k, rest], SV[:, k, rest], M[:, k])
                dve.drain()
                yield
                for t in range(tiles):
                    tt(X1[:, t].rearrange("p (a b) -> p a b", a=16), SV[:, 2 * t].unsqueeze(2).to_broadcast([rows, 16, 16]),
                       SV[:, 2 * t + 1].unsqueeze(1).to_broadcast([rows, 16, 16]), ALU.add)
                dve.drain()
                for t in range(tiles):
                    V.max(CT[:, t, best], X1[:, t])
                dve.drain()
                for t in range(tiles):
                    V.max_index(PO[:, t, best], CT[:, t, best], X1[:, t])
                    V.match_replace(X2[:, t], CT[:, t, best], X1[:, t], NEG)
                dve.drain()
                for t in range(tiles):
                    V.max(CT[:, t, rest], X2[:, t])
                dve.drain()
                tt(esh[0:rows, 0:tiles], CT, CT[:, :, 0:1].to_broadcast([rows, tiles, 16]), ALU.subtract).then_inc(cs_ok, 1)
                for t in range(tiles):
                    V.max_index(PO[:, t, rest], CT[:, t, rest], X2[:, t])
                dve.drain()
                yield
                ts(A[:, :, 0], PO, 4, None, ALU.logical_shift_right)
                ts(A[:, :, 1], PO, 15, None, ALU.bitwise_and)
                dve.drain()
                O4 = O.rearrange("p k (a b) -> p k a b", a=16)
                for k in range(K2):
                    tt(O4[:, k], A[:, k // 2, k % 2].unsqueeze(2).to_broadcast([rows, 16, 16]),
                       iota[0:rows].unsqueeze(1).to_broadcast([rows, 16, 16]), ALU.is_equal)
                dve.drain()
                for k in range(K2):
                    tt(O4[:, k], O4[:, k], SI[:, k].unsqueeze(1).to_broadcast([rows, 16, 16]), ALU.mult)
                dve.drain()
                for t in range(tiles):
                    V.reduce_sum(IA[:, 2 * t:2 * t + 2], O4[:, 2 * t:2 * t + 2], AX)
                dve.wait_ge(exp_ok, n + 1)
                V.reciprocal(RS, esum[0:rows, 0:tiles])
                dve.drain()
                for t in range(tiles):
                    ts(weights(t), EN[:, t], RS[:, t:t + 1])
                    stt(experts(t), IA[:, 2 * t], float(NKEY), IA[:, 2 * t + 1])
                dve.drain()
                yield

            def add_sums(i, t, rows):
                tt(acc[0:rows, t], PVf[0:rows], acc[0:rows, t], ALU.add).then_inc(add_ok, 1)

            def mean_square(i, rows):
                dve.wait_ge(sum_ok, i + 2)
                ts(ss2[0:rows], ss2[0:rows], 1.0 / D, EPS).then_inc(fm_ok, 1)

            def scale_y(i, t, rows):
                dve.wait_ge(fr_ok, i + 1)
                V.reciprocal(rt2[0:rows], rt2[0:rows])
                dve.drain()
                stt(acc[0:rows, t], acc[0:rows, t], rt2[0:rows, 0:1], nfin[0:rows], ALU.mult, ALU.mult).then_inc(yo_ok, 1)

            def batches(c):
                def dots(s):
                    if s % BT == 0:
                        dve.wait_ge(hnc_in[s // BT], 16 * (c + 1))
                        dve.sem_inc(dve_at, 1)
                    for k in range(4):
                        dve.wait_ge(u_in[k], 16 * (BC * c + s + 1))
                        u = uring[:, k, :]
                        V.tensor_tensor_reduce(out=u, in0=u, in1=hnc[:, s // BT], scale=1.0, scalar=0.0, op0=ALU.mult,
                                               op1=ALU.add, accum_out=dots_[:, s % 2, k:k + 1]).then_inc(u_used, 1)

                def weigh(b):
                    dve.wait_ge(gelu_ok, BC * c + b + 1)
                    tt(wt[:, b % 4], ac[:, b % 2], gc[:, 4 * b:4 * b + 4], ALU.mult).then_inc(w_ok, 1)

                def row(b):
                    t = b // BT
                    if b % BT == 0:
                        dve.wait_ge(acc_in[t], 16 * (c + 1))
                        dve.sem_inc(dve_at, 1)
                    s = 4 * (b % 2) + ONPE
                    dve.wait_ge(v_in[s], 16 * (BC // 2 * c + b // 2 + 1))
                    stt(acc[:, t], vring[:, s, :], wt[:, b % 4, ONPE:ONPE + 1], acc[:, t]).then_inc(v_dve, 1)

                for s in range(BS):
                    if s < BC:
                        dots(s)
                    if 1 <= s <= BC:
                        weigh(s - 1)
                    for t in range(2):
                        if s == BT * (t + 1) + 2:
                            dve.drain()
                            dve.wait_ge(v_pe, BC * c + BT * (t + 1) + 2)
                            add_sums(2 * c + t, t, P)
                        elif s == BT * (t + 1) + 3:
                            mean_square(2 * c + t, P)
                        elif s == BT * (t + 1) + 4:
                            scale_y(2 * c + t, t, P)
                    if 2 <= s <= BC + 1:
                        dve.drain()
                        row(s - 2)
                    yield

            def chunk(c, cp, last):
                n = N if last else C
                upto = interleaved(None if cp is None else batches(cp), [0])
                for q in range(QT):
                    upto(q // 2 + 1)
                    conv(c, q, last)
                if not last:
                    V.tensor_copy(xl[:, :, 0:3], xl[:, :, C:C + 3]).then_inc(halo_ok, 1)
                for j in range(SJ):
                    upto(AT_S5 + j)
                    s5(c, j)
                    if AT_S5 + j in [at_y(q) for q in range(QT)]:
                        y_tile(c, (j - 6) // 4)
                for q in range(QT):
                    upto(AT_LRU + q // 2)
                    lru(c, q, last)
                    if last and q == QT - 1:
                        dve.wait_ge(smp_mm, 4)
                        tt(hS.rearrange("p a b c -> p (a b c)"), pre.rearrange("p a b c -> p (a b c)"), SB[0][:, 0:2 * SJ * NS],
                           ALU.add).then_inc(smp_ok, 1)
                upto(at_y(QT - 1))
                y_tile(c, QT - 1)
                if last:
                    dve.wait_ge(smp_mm, 5)
                    for q in range(QT):
                        stt(yS[:, q, C:N], uS[:, q, C:N], dskip[:, q:q + 1], SB[1][:, NS * q:NS * q + NS])
                    dve.drain()
                    dve.sem_inc(smp_ok, 1)
                upto(AT_GLU)
                for q in range(QT):
                    dve.wait_ge(evac, EVACS * c + U_GLU + q + 1)
                    tt(uS[:, q, 0:n], yS[:, q, 0:n], rT[:, q, 0:n], ALU.mult).then_inc(a_ok, 1)
                for m in range(KT):
                    upto(AT_MIX + 2 * m // 3)
                    dve.wait_ge(unit, UNITS * c + U_MIX + m + 1)
                    A, B2 = ga[:, m, 0:n], gb[:, m, 0:n]
                    tt(A, MIXB[m % 2][0][:, 0:n], A, ALU.mult)
                    tt(B2, MIXB[m % 2][1][:, 0:n], B2, ALU.mult)
                    dve.drain()
                    tt(hT[:, m, 0:n], A, B2, ALU.add).then_inc(mix_ok, 1)
                upto(AT_X2)
                dve.wait_ge(unit, UNITS * c + U_Q)
                dve.wait_ge(tok_in, 16 * (2 * (c + 1) + (1 if last else 0)))
                for t, rn, r0 in rows_of(last):
                    for half in range(2):
                        v = x_tok[0:rn, t, 512 * half:512 * half + 512]
                        tt(v, OUTB[t][half][0:rn], v, ALU.add).then_inc(x2_ok, 1)
                upto(AT_HN)
                dve.wait_ge(sq2_ok, c + 1)
                for t, rn, r0 in rows_of(last):
                    ts(ss[0:rn, t:t + 1], ss[0:rn, t:t + 1], 1.0 / D, EPS)
                dve.drain()
                dve.sem_inc(ms2_ok, 1)
                dve.wait_ge(rt2_ok, c + 1)
                for t, rn, r0 in rows_of(last):
                    V.reciprocal(ss[0:rn, t:t + 1], ss[0:rn, t:t + 1])
                dve.drain()
                dve.wait_ge(x2_out, 16 * (2 * (c + 1) + (1 if last else 0)))
                dve.wait_ge(nf_in, 16 * (c + 2))
                for t, rn, r0 in rows_of(last):
                    stt(x_tok[0:rn, t, :], x_tok[0:rn, t, :], ss[0:rn, t:t + 1], nffn[0:rn], ALU.mult, ALU.mult).then_inc(hn_ok, 1)
                for h in range(HEADS):
                    upto(at_q(h))
                    dve.wait_ge(s_ev, HEADS * c + h + 1)
                    dve.sem_inc(dve_at, 1)
                    for third, _ in enumerate(topk(HEADS * c + h, P, 2, lambda t, h=h: gn[:, HEADS * t + h],
                                                   lambda t, h=h: idxn[:, HEADS * t + h])):
                        if third < 2:
                            upto(at_q(h) + third + 1)
                if last:
                    upto(AT_NORM)
                    dve.wait_ge(s8_in, 16)
                    for _ in topk(HEADS * CH, NS * HEADS, 1, lambda t: g8[0:NS * HEADS], lambda t: i8[0:NS * HEADS]):
                        pass
                    dve.sem_inc(i8_ok, 1)
                if not last:
                    upto(AT_NORM)
                    norm(c + 1, columns(c + 1))
                upto(BS)
                dve.drain()
                V.tensor_copy(idxc, flat(idxn))
                V.tensor_copy(gc, flat(gn))
                dve.drain()
                dve.sem_inc(idx_ok, 1)

            chunk(0, None, False)
            with dve.Fori(0, CH - 2) as cp:
                chunk(cp + 1, cp, False)
            chunk(CH - 1, CH - 2, True)
            for _ in batches(CH - 1):
                pass
            NB = BC * CH
            dve.wait_ge(hnS_in, 16 * NS)
            for h in range(HEADS):
                dve.wait_ge(u_in[h % 4], 16 * (NB + h // 4 + 1))
                u = uring[:, h % 4, :]
                V.tensor_tensor_reduce(out=u, in0=u, in1=hnc[:, 0], scale=1.0, scalar=0.0, op0=ALU.mult,
                                       op1=ALU.add, accum_out=accS[:, h:h + 1]).then_inc(u_used, 1)
            dve.wait_ge(gelu_ok, NB + 1)
            dve.wait_ge(sc_in, 32)
            tt(wS, acS, gS, ALU.mult)
            dve.drain()
            tt(w8, wS.unsqueeze(2).to_broadcast([P, HEADS, NS]), mk2.unsqueeze(1).to_broadcast([P, HEADS, NS]),
               ALU.mult).then_inc(w8_ok, 1)
            dve.wait_ge(pv_ok, 1)
            dve.wait_ge(acc_in[0], 16 * (CH + 1))
            add_sums(TILES, 0, NS)
            mean_square(TILES, NS)
            scale_y(TILES, 0, NS)

        @block.tensor
        def _(pe):
            mm = nc.tensor.matmul

            def norm(c, n):
                need(pe, s_ev, HEADS * c)
                pe.wait_ge(sq_ok, c + 1)
                for k in range(KT):
                    ins = mm(YB[0][:, 0:n], ones, ga[:, k, 0:n], start=(k == 0), stop=(k == KT - 1))
                ins.then_inc(ss_ok, 1)

            def slot(c, l):
                pe.wait_ge(slot_in[l % RING], 16 * (SLOTS // RING * c + l // RING + 1))
                return ring[:, l % RING, :]

            def project(c, u, l, rhs, k, n):
                w = slot(c, l)
                e = u if u < U_MIX else u - 16
                if u not in (U_Q, U_Q + 1):
                    need(pe, evac, EVACS * c + e - 1)
                for t in range(k):
                    ins = mm(PB[u % 2][:, 0:n], w[:, P * t:P * t + P], rhs[:, t, 0:n], start=(t == 0), stop=(t == k - 1))
                ins.then_inc(unit, 1)

            def s5_in(c, j):
                o = 32 * (j % 4)
                if j >= 2:
                    pe.wait_ge(bu_read, SJ * c + j - 1)
                pe.wait_ge(evac, EVACS * c + U_U + j // 4 + 1)
                for part in range(2):
                    ins = mm(SB[j % 2][:, C * part:C * part + C], bT[o:o + 32, part, j // 4], uS[o:o + 32, j // 4, 0:C],
                             start=True, stop=True)
                ins.then_inc(bu_ok, 1)

            def s5_out(c, j):
                o, q = 32 * (j % 4), j // 4
                pe.wait_ge(h_ok, SJ * c + j + 1)
                if j % 4 == 0 and q >= 2:
                    pe.wait_ge(y_ok, QT * c + q - 1)
                for part in range(2):
                    ins = mm(YB[q % 2][o:o + 32, 0:C], cT[:, part, j], hb[:, j % 3, part], start=(part == 0), stop=(part == 1))
                ins.then_inc(y_mm, 1)

            def batches(c):
                for s in range(BS):
                    if 2 <= s <= BC + 1:
                        b = s - 2
                        if b % BT == 0:
                            pe.wait_ge(sum_ok, 2 * c + b // BT + 1)
                        pe.wait_ge(dg_ok, BC * c + b + 1)
                        for k in range(ONPE):
                            r = 4 * (b % 2) + k
                            pe.wait_ge(v_in[r], 16 * (BC // 2 * c + b // 2 + 1))
                            for half in range(2):
                                ins = mm(PV[:, half], dg[:, ONPE * (b % 2) + k], vring[:, r, 512 * half:512 * half + 512],
                                         start=(b % BT == 0 and k == 0), stop=(b % BT == BT - 1 and k == ONPE - 1))
                        ins.then_inc(v_pe, 1)
                    yield

            def chunk(c, cp, last):
                n = N if last else C
                upto = interleaved(None if cp is None else batches(cp), [0])
                pe.wait_ge(hT_ok, KT * (c + 1))
                for u in range(U_GATE):
                    upto(u // 2)
                    project(c, u, u, hT, KT, n)
                upto(AT_GATE)
                for u in range(U_GATE, U_GA):
                    q, s = divmod(u - U_GATE, 2)
                    if s == 0:
                        pe.wait_ge(conv_ok, QT * c + q + 1)
                    pe.wait_ge(evac, EVACS * c + u - 1)
                    mm(PB[u % 2][:, 0:n], bd[:, q, s], xc[:, q, 0:n], start=True, stop=True).then_inc(unit, 1)
                if isinstance(c, int) and c == 0:
                    pe.wait_ge(bp_ok, 2)
                for m in range(2 * KT):
                    upto(AT_S5 + m)
                    s5_in(c, m)
                    project(c, U_GA + m, U_YL + 4 + m, hT, KT, n)
                    if m >= 2:
                        s5_out(c, m - 2)
                upto(AT_S5 + SJ)
                s5_out(c, SJ - 2)
                s5_out(c, SJ - 1)
                if last:
                    pe.wait_ge(bu_read, SJ * (c + 1))
                    for r in range(4):
                        if r:
                            pe.wait_ge(smp_mm, r)
                        for part in range(2):
                            for j in range(r, SJ, 4):
                                at = NS * (SJ * part + j)
                                ins = mm(SB[0][:, at:at + NS], bT[32 * r:32 * r + 32, part, j // 4],
                                         uS[32 * r:32 * r + 32, j // 4, C:N], start=True, stop=True)
                        ins.then_inc(smp_mm, 1)
                    upto(at_y(QT - 1))
                    pe.wait_ge(smp_ok, 1)
                    for j in range(SJ):
                        o, q = 32 * (j % 4), j // 4
                        for part in range(2):
                            ins = mm(SB[1][o:o + 32, NS * q:NS * q + NS], cT[:, part, j], hS[:, part, j],
                                     start=(part == 0), stop=(part == 1))
                    ins.then_inc(smp_mm, 1)
                upto(AT_GLU)
                pe.wait_ge(z_ok, QT * (c + 1) + (1 if last else 0))
                for q in range(QT):
                    project(c, U_GLU + q, 28 + q, yS, QT, n)
                for m in range(KT):
                    upto(AT_MIX + 2 * m // 3)
                    w = slot(c, 32 + m)
                    if m == 0:
                        pe.wait_ge(lru_ok, QT * (c + 1))
                        pe.wait_ge(y_ok, QT * (c + 1))
                        pe.wait_ge(a_ok, QT * (c + 1))
                    if m >= 2:
                        pe.wait_ge(mix_ok, KT * c + m - 1)
                    for side, src in ((1, gy), (0, uS)):
                        for t in range(QT):
                            ins = mm(MIXB[m % 2][side][:, 0:n], w[:, 512 * side + P * t:512 * side + P * t + P],
                                     src[:, t, 0:n], start=(t == 0), stop=(t == QT - 1))
                    ins.then_inc(unit, 1)
                for k in range(KT):
                    upto(AT_OUT + 2 * k // 3)
                    w = slot(c, 40 + k)
                    if k == 0:
                        pe.wait_ge(evac, EVACS * c + U_MIX)
                        pe.wait_ge(mix_ok, KT * (c + 1))
                    for t, rn, r0 in rows_of(last):
                        for half in range(2):
                            ins = mm(OUTB[t][half][0:rn], hT[:, k, r0:r0 + rn], w[:, 512 * half:512 * half + 512],
                                     start=(k == 0), stop=(k == KT - 1))
                    ins.then_inc(unit, 1)
                upto(AT_TR)
                pe.wait_ge(hn_ok, 2 * (c + 1) + (1 if last else 0))
                for t, rn, r0 in rows_of(last):
                    for k in range(KT):
                        if t == 2:
                            dst = psum[:, 0, NS * k:NS * k + NS]
                        else:
                            dst = psum[:, 2 + 2 * t + k // 4, P * (k % 4):P * (k % 4) + P]
                        ins = nc.tensor.transpose(dst, x_tok[0:rn, t, P * k:P * k + P], ident[0:rn, 0:rn])
                ins.then_inc(tr_ok, 1)
                pe.wait_ge(tr_ev, c + 1)
                for h in range(HEADS):
                    upto(at_q(h))
                    for s in range(2):
                        project(c, U_Q + 2 * h + s, 48 + 2 * h + s, gb, KT, n)
                    pe.wait_ge(evac, EVACS * c + 40 + 2 * h + 2)
                    pe.wait_ge(key_in[h % 2], 16 * (HEADS // 2 * c + h // 2 + 1))
                    if h >= 2:
                        pe.wait_ge(s_ev, HEADS * c + h - 1)
                    for t, rn, r0 in rows_of(last):
                        for s in range(2):
                            dst = SB[h % 2][0:rn, NKEY * s:NKEY * s + NKEY] if t == 2 else \
                                YB[h % 2][:, NKEY * (2 * t + s):NKEY * (2 * t + s) + NKEY]
                            ins = mm(dst, qT[:, s, r0:r0 + rn], kb[:, h % 2, s], start=True, stop=True)
                    ins.then_inc(s_mm, 1)
                if not last:
                    upto(AT_NORM)
                    norm(c + 1, columns(c + 1))
                upto(BS)

            pe.wait_ge(const_ok, 6)
            norm(0, C)
            pe.wait_ge(bp_ok, 1)
            for part in range(2):
                for j in range(SJ):
                    o = 32 * (j % 4)
                    ins = mm(SB[part][o:o + 32, P * (j // 4):P * (j // 4) + P], bp[:, part, j], ident,
                             start=True, stop=True)
            ins.then_inc(bt_mm, 1)
            pe.wait_ge(bd_in, 16)
            pe.wait_ge(par_in, 16 * 12)
            pe.sem_inc(v_pe, 2)
            chunk(0, None, False)
            with pe.Fori(0, CH - 2) as cp:
                chunk(cp + 1, cp, False)
            chunk(CH - 1, CH - 2, True)
            for _ in batches(CH - 1):
                pass
            NB = BC * CH
            pe.wait_ge(sum_ok, TILES + 1)
            pe.wait_ge(w8_ok, 1)
            for h in range(HEADS):
                pe.wait_ge(v_in[h], 16 * (NB // 2 + 1))
                for half in range(2):
                    ins = mm(PV[0:NS, half], w8[:, h], vring[:, h, 512 * half:512 * half + 512],
                             start=(h == 0), stop=(h == HEADS - 1))
            ins.then_inc(pv_ok, 1)


def kernel(**inputs):
    import concourse.bacc as bacc
    from concourse.bass_utils import run_bass_kernel_spmd

    a = {k: np.asarray(v) for k, v in inputs.items()}
    x = np.concatenate([a["x_prompt"][0], a["x_sample"][:, 0]], axis=0)

    def states(v):
        v = v.reshape((SJ, 2, 64) + v.shape[2:])
        return np.moveaxis(v, 0, 2).reshape((P, SJ) + v.shape[3:])

    def chans(v):
        v = v.reshape(v.shape[:-1] + (-1, P))
        return np.moveaxis(np.moveaxis(v, -1, 0), -1, 1)

    def tiles(w):
        k, m = w.shape
        return w.reshape(k // P, P, m // P, P).transpose(2, 1, 0, 3).reshape(m // P, P, k)

    w_in = tiles(a["w_in"][0])
    order = list(range(4, 8)) + list(range(0, 4)) + list(range(8, 28))
    gate = np.stack([a["lru_w_a"][0], a["lru_w_x"][0]])
    bd = np.zeros((P, QT, 2, P), np.float32)
    c_raw = np.zeros((P, 2, SJ, 32), np.float32)
    c_all = [states(a[n][0].transpose(0, 2, 1)) for n in ("s5_c_re", "s5_c_im")]
    for g2 in range(2):
        r = slice(64 * g2, 64 * g2 + 64)
        bd[r, :, :, r] = gate[:, g2::2].transpose(2, 1, 0, 3)
        for s in range(2):
            c_raw[r, s, :, 16 * g2:16 * g2 + 16] = c_all[s][r]
    conv_w = a["conv_w"][0]
    prm = np.concatenate([chans(a["conv_b"][0]), chans(a["s5_d"][0]), chans(a["s5_b_glu"][0]),
                          chans(a["lru_b_a"][0].reshape(-1)), chans(a["lru_b_x"][0].reshape(-1)),
                          chans(a["lru_lam"][0].reshape(-1)), np.zeros((P, QT), np.float32)]
                         + [chans(conv_w[k]) for k in range(3)], axis=1)
    ins = {
        "xT": chans(x), "x_tok": x, "w_in": w_in[order], "w_glu": tiles(a["s5_w_glu"][0]),
        "w_ab": np.concatenate([tiles(a["w_proj_a"][0]), tiles(a["w_proj_b"][0])], axis=2),
        "w_out": a["w_out"][0].reshape(KT, P, D),
        "lam_re": states(a["s5_lam_re"][0]), "lam_im": states(a["s5_lam_im"][0]),
        "log_dt": a["s5_log_dt"][0].reshape(SJ, 2).T,
        "b_raw": np.stack([states(a["s5_b_re"][0]), states(a["s5_b_im"][0])], axis=1),
        "c_raw": c_raw,
        "s5_0": np.stack([states(np.moveaxis(a[n][0], 0, 2)) for n in ("state_s5_re", "state_s5_im")], axis=1),
        "prm": prm, "convw3": chans(conv_w[3]), "nmix": chans(a["norm_mix"][0]),
        "sconv": chans(a["state_conv"][0].transpose(1, 0, 2)), "slru": chans(a["state_lru_h"][0]),
        "lru_bd": bd,
        "w_q": tiles(a["peer_w_q"][0]),
        "keys": a["peer_keys"][0].reshape(2 * HEADS, NKEY, P).transpose(2, 0, 1),
        "u": a["peer_u"][0], "v": a["peer_v"][0],
        "norm_ffn": a["norm_ffn"][0], "norm_final": a["norm_final"],
    }
    ins = {f"in_{k}": np.ascontiguousarray(v) for k, v in ins.items()}
    outs = {"y_prompt": (SEQ, D), "y_sample": (NS, D), "s5_s": (P, 2, SJ, NS), "s5_p": (P, 2, SJ),
            "lru_p": (P, QT), "lru_s": (P, QT, NS), "conv_p": (P, QT, 3), "conv_s": (P, QT, 3, NS)}
    nc = bacc.Bacc("TRN2", target_bir_lowering=False, num_devices=1)
    i_ = {k[3:]: nc.dram_tensor(k, v.shape, F32, kind="ExternalInput").ap() for k, v in ins.items()}
    o_ = {k: nc.dram_tensor(f"out_{k}", s, F32, kind="ExternalOutput").ap() for k, s in outs.items()}
    build(nc, i_, o_)
    res = run_bass_kernel_spmd(nc, [ins], core_ids=[0]).results[0]
    r = {k: np.asarray(res[f"out_{k}"]) for k in outs}

    def unstate(v):
        v = v.reshape((2, 64, SJ) + v.shape[2:])
        return np.moveaxis(v, 2, 0).reshape((32, 64) + v.shape[3:])

    s5p = [unstate(r["s5_p"][:, s])[None, None] for s in range(2)]
    s5s = [np.moveaxis(unstate(r["s5_s"][:, s]), 2, 0)[None] for s in range(2)]
    return (r["y_prompt"][None], r["y_sample"][:, None], s5p[0], s5p[1],
            r["lru_p"].T.reshape(1, 1, DB), r["conv_p"].transpose(2, 1, 0).reshape(1, 1, 3, DB),
            s5s[0], s5s[1], r["lru_s"].transpose(2, 1, 0).reshape(1, NS, DB),
            r["conv_s"].transpose(3, 2, 1, 0).reshape(1, NS, 3, DB))
```
